# Optimizing a Trainium2 kernel written in Bass

```python
import math
import jax, jax.numpy as jnp
from jax import lax
import numpy as np

D_MODEL = 1024
BATCH = 1
SEQ = 256
DEPTH = 1
DEC_BATCH = 1
DEC_SEQ = 1024
PAST_LEN = 128

D_RNN = D_MODEL // 2
N_RNN_HEADS = 8
RNN_HEAD_DIM = D_RNN // N_RNN_HEADS
CONV_RNN_WIDTH = 4
LRU_C = 8.0
D_CONV = D_MODEL // 2
CONV_WIDTH = 31
D_IN = 2 * D_RNN + 2 * D_CONV
N_MEM = 256
N_XHEADS = 4
XHEAD_DIM = D_MODEL // N_XHEADS
N_PEER_HEADS = 8
N_KEYS = 128
N_EXPERTS = N_KEYS * N_KEYS
PEER_TOPK = 16
D_QUERY = 256
D_SUBKEY = D_QUERY // 2
PEER_BLOCK = 128
EPS = 1e-6

kernel_name = "hybrid_rglru_conformer_peer_encoder"

def rmsnorm(x, g):
    xf = x.astype(jnp.float32)
    y = xf * lax.rsqrt(jnp.mean(xf * xf, axis=-1, keepdims=True) + EPS)
    return (y * g.astype(jnp.float32)).astype(x.dtype)

def layernorm(x, g, b):
    xf = x.astype(jnp.float32)
    mu = jnp.mean(xf, axis=-1, keepdims=True)
    var = jnp.mean(jnp.square(xf - mu), axis=-1, keepdims=True)
    y = (xf - mu) * lax.rsqrt(var + EPS)
    return (y * g.astype(jnp.float32) + b.astype(jnp.float32)).astype(x.dtype)

def depthwise_conv(x, w, b, pad):
    C = x.shape[-1]
    y = lax.conv_general_dilated(x, w[:, None, :].astype(x.dtype), window_strides=(1,),
                                 padding=[pad], dimension_numbers=('NWC', 'WIO', 'NWC'),
                                 feature_group_count=C)
    return y + b.astype(x.dtype)

def _lin_comb(c1, c2):
    a1, b1 = c1
    a2, b2 = c2
    return a1 * a2, a2 * b1 + b2

def rg_lru_bidir(x, w_a, b_a, w_x, b_x, lam):
    B, S, _ = x.shape
    xh = x.reshape(B, S, N_RNN_HEADS, RNN_HEAD_DIM)
    r = jax.nn.sigmoid((jnp.einsum('bshi,zhij->zbshj', xh, w_a) + b_a[:, None, None]).astype(jnp.float32))
    i = jax.nn.sigmoid((jnp.einsum('bshi,zhij->zbshj', xh, w_x) + b_x[:, None, None]).astype(jnp.float32))
    r = r.reshape(2, B, S, D_RNN)
    i = i.reshape(2, B, S, D_RNN)
    log_a = LRU_C * r * jax.nn.log_sigmoid(lam.astype(jnp.float32))[:, None, None, :]
    a = jnp.exp(log_a)
    mult = jnp.sqrt(jnp.maximum(-jnp.expm1(2.0 * log_a), 0.0))
    u = mult * i * x.astype(jnp.float32)[None]
    _, h_f = lax.associative_scan(_lin_comb, (a[0], u[0]), axis=1)
    _, h_b = lax.associative_scan(_lin_comb, (a[1], u[1]), axis=1, reverse=True)
    return (h_f + h_b).astype(x.dtype)

def mixer(x, g_mix, w_in, conv4_w, conv4_b, lru_wa, lru_ba, lru_wx, lru_bx, lru_lam,
          conv31_w, conv31_b, conv_ln_g, conv_ln_b, g_out_rnn, g_out_conv, w_out):
    h = rmsnorm(x, g_mix)
    z = h @ w_in
    x_rnn, g_rnn, glu_a, glu_b = jnp.split(z, [D_RNN, 2 * D_RNN, 2 * D_RNN + D_CONV], axis=-1)
    xr = depthwise_conv(x_rnn, conv4_w, conv4_b, (CONV_RNN_WIDTH // 2, CONV_RNN_WIDTH - 1 - CONV_RNN_WIDTH // 2))
    y_rnn = rg_lru_bidir(xr, lru_wa, lru_ba, lru_wx, lru_bx, lru_lam) * jax.nn.gelu(g_rnn)
    c = glu_a * jax.nn.sigmoid(glu_b)
    c = depthwise_conv(c, conv31_w, conv31_b, (CONV_WIDTH // 2, CONV_WIDTH // 2))
    c = jax.nn.silu(layernorm(c, conv_ln_g, conv_ln_b))
    o = jnp.concatenate([rmsnorm(y_rnn, g_out_rnn), rmsnorm(c, g_out_conv)], axis=-1)
    return o @ w_out

def mem_cross_attn(x, mem, g_xattn, g_mem, w_xq, w_xkv, w_xo):
    B, S, _ = x.shape
    M = mem.shape[1]
    h = rmsnorm(x, g_xattn)
    m = rmsnorm(mem, g_mem)
    q = (h @ w_xq).reshape(B, S, N_XHEADS, XHEAD_DIM)
    k, v = jnp.split(m @ w_xkv, 2, axis=-1)
    k = k.reshape(B, M, N_XHEADS, XHEAD_DIM)
    v = v.reshape(B, M, N_XHEADS, XHEAD_DIM)
    s = jnp.einsum('bshd,bmhd->bhsm', q, k).astype(jnp.float32) * (1.0 / math.sqrt(XHEAD_DIM))
    p = jax.nn.softmax(s, axis=-1).astype(v.dtype)
    o = jnp.einsum('bhsm,bmhd->bshd', p, v).reshape(B, S, D_MODEL)
    return o @ w_xo

def peer(x, g_peer, w_pq, sub_keys, u_tab, v_tab):
    B, S, D = x.shape
    T = B * S
    h = rmsnorm(x, g_peer).reshape(T, D)
    q = (h @ w_pq).reshape(T, N_PEER_HEADS, 2, D_SUBKEY)
    s = jnp.einsum('thpk,hpnk->thpn', q, sub_keys).astype(jnp.float32)
    sv, si = lax.top_k(s, PEER_TOPK)
    cand = (sv[:, :, 0, :, None] + sv[:, :, 1, None, :]).reshape(T, N_PEER_HEADS, PEER_TOPK * PEER_TOPK)
    cand_idx = (si[:, :, 0, :, None] * N_KEYS + si[:, :, 1, None, :]).reshape(T, N_PEER_HEADS, PEER_TOPK * PEER_TOPK)
    cv, ci = lax.top_k(cand, PEER_TOPK)
    eidx = jnp.take_along_axis(cand_idx, ci, axis=-1)
    gate = jax.nn.softmax(cv, axis=-1)
    nb = T // PEER_BLOCK
    hb = h.reshape(nb, PEER_BLOCK, D)
    ib = eidx.reshape(nb, PEER_BLOCK, N_PEER_HEADS * PEER_TOPK)
    gb = gate.reshape(nb, PEER_BLOCK, N_PEER_HEADS * PEER_TOPK)

    def block(args):
        xb, idx, g = args
        ub = jnp.take(u_tab, idx, axis=0)
        vb = jnp.take(v_tab, idx, axis=0)
        act = jax.nn.gelu(jnp.einsum('td,tkd->tk', xb, ub).astype(jnp.float32)) * g
        return jnp.einsum('tk,tkd->td', act.astype(xb.dtype), vb)

    out = lax.map(block, (hb, ib, gb))
    return out.reshape(B, S, D)

def encode(x, mem, params):
    (g_mix, w_in, conv4_w, conv4_b, lru_wa, lru_ba, lru_wx, lru_bx, lru_lam,
     conv31_w, conv31_b, conv_ln_g, conv_ln_b, g_out_rnn, g_out_conv, w_out,
     g_xattn, g_mem, w_xq, w_xkv, w_xo,
     g_peer, w_pq, peer_sub_keys, peer_u, peer_v, g_final) = params
    for l in range(DEPTH):
        x = x + mixer(x, g_mix[l], w_in[l], conv4_w[l], conv4_b[l], lru_wa[l], lru_ba[l], lru_wx[l],
                      lru_bx[l], lru_lam[l], conv31_w[l], conv31_b[l], conv_ln_g[l], conv_ln_b[l],
                      g_out_rnn[l], g_out_conv[l], w_out[l])
        x = x + mem_cross_attn(x, mem, g_xattn[l], g_mem[l], w_xq[l], w_xkv[l], w_xo[l])
        x = x + peer(x, g_peer[l], w_pq[l], peer_sub_keys[l], peer_u[l], peer_v[l])
    return rmsnorm(x, g_final)

def setup_inputs(seed: int = 0) -> dict:
    key = jax.random.key(seed)
    ks = iter(jax.random.split(key, 48))
    f32 = jnp.float32

    def nrm(shape, scale):
        return jax.random.normal(next(ks), shape, f32) * scale

    def gain(shape):
        return 1.0 + 0.01 * jax.random.normal(next(ks), shape, f32)

    L = DEPTH
    a8 = jax.random.uniform(next(ks), (L, 2, D_RNN), f32, 0.9, 0.999)
    s = a8 ** (1.0 / LRU_C)
    lam = jnp.log(s) - jnp.log1p(-s)
    return {
        "x_prompt": nrm((BATCH, SEQ, D_MODEL), 1.0),
        "x_sample": nrm((DEC_BATCH, DEC_SEQ, D_MODEL), 1.0),
        "mem_prompt": nrm((BATCH, N_MEM, D_MODEL), 1.0),
        "mem_sample": nrm((DEC_BATCH, N_MEM, D_MODEL), 1.0),
        "g_mix": gain((L, D_MODEL)),
        "w_in": nrm((L, D_MODEL, D_IN), D_MODEL ** -0.5),
        "conv4_w": nrm((L, CONV_RNN_WIDTH, D_RNN), CONV_RNN_WIDTH ** -0.5),
        "conv4_b": nrm((L, D_RNN), 0.01),
        "lru_wa": nrm((L, 2, N_RNN_HEADS, RNN_HEAD_DIM, RNN_HEAD_DIM), RNN_HEAD_DIM ** -0.5),
        "lru_ba": nrm((L, 2, N_RNN_HEADS, RNN_HEAD_DIM), 0.01),
        "lru_wx": nrm((L, 2, N_RNN_HEADS, RNN_HEAD_DIM, RNN_HEAD_DIM), RNN_HEAD_DIM ** -0.5),
        "lru_bx": nrm((L, 2, N_RNN_HEADS, RNN_HEAD_DIM), 0.01),
        "lru_lam": lam,
        "conv31_w": nrm((L, CONV_WIDTH, D_CONV), CONV_WIDTH ** -0.5),
        "conv31_b": nrm((L, D_CONV), 0.01),
        "conv_ln_g": gain((L, D_CONV)),
        "conv_ln_b": nrm((L, D_CONV), 0.01),
        "g_out_rnn": gain((L, D_RNN)),
        "g_out_conv": gain((L, D_CONV)),
        "w_out": nrm((L, D_RNN + D_CONV, D_MODEL), (D_RNN + D_CONV) ** -0.5),
        "g_xattn": gain((L, D_MODEL)),
        "g_mem": gain((L, D_MODEL)),
        "w_xq": nrm((L, D_MODEL, D_MODEL), D_MODEL ** -0.5),
        "w_xkv": nrm((L, D_MODEL, 2 * D_MODEL), D_MODEL ** -0.5),
        "w_xo": nrm((L, D_MODEL, D_MODEL), D_MODEL ** -0.5),
        "g_peer": gain((L, D_MODEL)),
        "w_pq": nrm((L, D_MODEL, N_PEER_HEADS * D_QUERY), D_MODEL ** -0.5),
        "peer_sub_keys": nrm((L, N_PEER_HEADS, 2, N_KEYS, D_SUBKEY), D_SUBKEY ** -0.5),
        "peer_u": nrm((L, N_EXPERTS, D_MODEL), D_MODEL ** -0.5),
        "peer_v": nrm((L, N_EXPERTS, D_MODEL), 0.5),
        "g_final": gain((D_MODEL,)),
    }

def reference(x_prompt, x_sample, mem_prompt, mem_sample,
              g_mix, w_in, conv4_w, conv4_b, lru_wa, lru_ba, lru_wx, lru_bx, lru_lam,
              conv31_w, conv31_b, conv_ln_g, conv_ln_b, g_out_rnn, g_out_conv, w_out,
              g_xattn, g_mem, w_xq, w_xkv, w_xo,
              g_peer, w_pq, peer_sub_keys, peer_u, peer_v, g_final):
    params = (g_mix, w_in, conv4_w, conv4_b, lru_wa, lru_ba, lru_wx, lru_bx, lru_lam,
              conv31_w, conv31_b, conv_ln_g, conv_ln_b, g_out_rnn, g_out_conv, w_out,
              g_xattn, g_mem, w_xq, w_xkv, w_xo,
              g_peer, w_pq, peer_sub_keys, peer_u, peer_v, g_final)
    y_prompt = encode(x_prompt, mem_prompt, params)
    y_sample = encode(x_sample, mem_sample, params)
    return (y_prompt, y_sample)


_drawn_inputs = setup_inputs


def setup_inputs(seed=0):
    import zlib

    import numpy as np

    out = dict(_drawn_inputs(seed))
    spreads = {}
    factors = {'g_mix': 2.683,
     'lru_ba': 8.0,
     'lru_bx': 6.61,
     'conv31_b': 2.733,
     'conv_ln_g': 3.535,
     'conv_ln_b': 3.858,
     'g_out_rnn': 3.867,
     'g_out_conv': 3.932,
     'g_xattn': 8.0,
     'g_mem': 8.0,
     'g_peer': 22.488,
     'g_final': 30.602}
    for name, (base, spread) in spreads.items():
        noise = np.random.default_rng([zlib.crc32(name.encode()), seed]).standard_normal(out[name].shape)
        drawn = base * np.exp(spread * noise) if base else spread * noise
        out[name] = __import__('jax').numpy.asarray(drawn.astype(out[name].dtype))
    for name, factor in factors.items():
        out[name] = (out[name] * factor).astype(out[name].dtype)
    return out
```

```python
import concourse.bass as bass
from concourse import mybir
from contextlib import ExitStack

P = 128
D = 1024
KD = D // P
SEQ0, SEQ1 = 256, 1024
T = SEQ0 + SEQ1
NB = T // P
NB0 = SEQ0 // P
NMEM = 256
MB = 2 * NMEM // P
CH = 4
TAPS4, TAPS31 = 4, 31
NH = 4
PH = 8
NK = 128
TOPK = 16
PICKS = PH * TOPK
EPS = 1e-6
BANK = 512

A4, B4 = 2, 2 + SEQ0 + 2
L4 = SEQ0 + 2 + SEQ1
O4 = SEQ0 + 2
A31, B31 = 15, 15 + SEQ0 + 15
L31 = SEQ0 + 15 + SEQ1
O31 = SEQ0 + 15
PITCH = L31 + 30
TP = L31 + 1

COLS = [("g_mix", KD), ("g_mem", KD), ("g_xattn", KD), ("g_peer", KD), ("conv4_w", TAPS4 * CH),
        ("conv4_b", CH), ("ba", 2 * CH), ("bx", 2 * CH), ("lam", 2 * CH), ("conv31_w", TAPS31 * CH),
        ("conv31_b", CH), ("ln_g", CH), ("ln_b", CH), ("g_rnn", CH), ("g_conv", CH)]
COL = {}
NCOL = 0
for _n, _w in COLS:
    COL[_n] = NCOL
    NCOL += _w

CHUNKS = [("x", 0), ("x", 1), ("x", 2), ("x", 3), ("g", 0), ("b", 0), ("a", 0), ("g", 1),
          ("b", 1), ("a", 1), ("g", 2), ("b", 2), ("a", 2), ("g", 3), ("b", 3), ("a", 3)]
BASE = {"x": 0, "g": CH, "a": 2 * CH, "b": 3 * CH}
Z_ITEMS, K_ITEMS, V_ITEMS, W_ITEMS = 8, 4, 4, 8
ITEMS = Z_ITEMS + K_ITEMS + V_ITEMS + W_ITEMS

JOBS = []
for _kind, _c in CHUNKS:
    JOBS.append(("z", _kind, _c))
    if _kind == "a":
        JOBS += [("gate", w, d, _c) for d in range(2) for w in "ax"]

R = 4
SLOTS = 16
PER = PICKS // SLOTS


def taker(job):
    return "dve" if job[:2] == ("z", "a") else "act"


def taken_before(n, engine):
    return sum(taker(j) == engine for j in JOBS[:n])


def build(nc, a, stop_at_x1=False):
    f32, u32 = mybir.dt.float32, mybir.dt.uint32
    ALU, ACT = mybir.AluOpType, mybir.ActivationFunctionType
    X = mybir.AxisListType.X
    ds = bass.ds

    kt_d = nc.dram_tensor("kt_scratch", (2, P, KD, NMEM), f32).ap()
    v_d = nc.dram_tensor("v_scratch", (2, P, 2, D), f32).ap()
    wp_d = nc.dram_tensor("wp_scratch", (P, KD, 2 * PH * NK), f32).ap()
    x1_d = a["out"] if stop_at_x1 else nc.dram_tensor("x1_scratch", (T, D), f32).ap()
    x2_d = nc.dram_tensor("x2_scratch", (T, D), f32).ap()

    ctx = ExitStack()
    with ctx:
        def sb(name, cols, dt=f32):
            return ctx.enter_context(nc.sbuf_tensor(name, [P, cols], dt))

        def sem(name):
            return ctx.enter_context(nc.semaphore(name))

        cols = sb("cols", NCOL)
        c_half = sb("c_half", 8 * CH)
        ident, ones512 = sb("ident", P), sb("ones512", P)
        small = sb("small", 64)
        arena = sb("arena", 51444)
        ps = ctx.enter_context(nc.psum_tensor("ps", [P, 8 * BANK], f32))
        at = [0]

        def piece(words, dt=f32):
            s = arena[:, at[0]:at[0] + words]
            at[0] += words
            return s if dt == f32 else s.bitcast(dt)

        HT = piece(KD * T)
        XP = piece(CH * PITCH)
        GG = piece(CH * TP)
        XS = piece(2 * D)
        zone_d = at[0]
        CI = piece(CH * PITCH)
        TH, TQ, A2, TX, AF, AB = (piece(TP) for _ in range(6))
        XR = piece(2 * TP)
        MT = piece(KD * MB * P)
        RING = piece(2 * 2 * D)
        GM = piece(16 * P)
        TB = piece(TP)
        hT = HT.rearrange("p (k t) -> p k t", k=KD)
        mT = MT.rearrange("p (k t) -> p k t", k=KD)
        wo_mix = HT[:, 0:KD * D].rearrange("p (k n) -> p k n", k=KD)
        gm = GM.rearrange("p (m n) -> p m n", m=16)
        xn_p0 = [XS[:, 0:D], XS[:, D:2 * D], TH[:, 0:D], TQ[:, 0:D]]
        sq_rnn = [TH, TQ, A2, TX]

        def xp(c, lo, n):
            return XP[:, c * PITCH + lo:c * PITCH + lo + n]

        def ci(c, lo, n):
            return CI[:, c * PITCH + lo:c * PITCH + lo + n]

        def gg(c, lo, n):
            return GG[:, c * TP + lo:c * TP + lo + n]

        def xr(c, lo, n):
            return XR[:, (c % 2) * TP + lo:(c % 2) * TP + lo + n]

        at[0] = 0
        WO = piece(KD * D)
        GR = piece(R * 2 * D)
        HN, HC, XC, AC, BC = (piece(D) for _ in range(5))
        SI, CI16 = piece(2 * PH * TOPK, u32), piece(PICKS, u32)
        IDXN, IDXC, GATN, GATC = piece(PICKS, u32), piece(PICKS, u32), piece(PICKS), piece(PICKS)
        assert at[0] <= zone_d
        at[0] = zone_d
        WP = piece(KD * 2 * PH * NK)
        WQ = piece(KD * D)
        KT = piece(KD * NMEM)
        VT = piece(2 * D)
        assert at[0] <= 51444
        diag = sb("diag", R * P)
        iota = sb("iota", TOPK)
        st = sb("st", R, u32)
        dots, acts = sb("dots", R), sb("acts", R)
        ring = [GR[:, r * 2 * D:(r + 1) * 2 * D] for r in range(R)]
        wo = WO.rearrange("p (k n) -> p k n", k=KD)
        wq = WQ.rearrange("p (k n) -> p k n", k=KD)
        wp = WP.rearrange("p (k n) -> p k n", k=KD)
        kt = KT.rearrange("p (k n) -> p k n", k=KD)
        vt = VT.rearrange("p (k n) -> p k n", k=2)
        SV, SIF = XC[:, 0:256], XC[:, 256:512]
        CV, I0, I1, E0 = (XC[:, 512 + i * 128:640 + i * 128] for i in range(4))
        CAND = arena[:, KD * D + R * 2 * D + 3 * D:KD * D + R * 2 * D + 5 * D]

        def bank(b, n=1):
            return ps[:, b * BANK:(b + n) * BANK]

        ACC, JUNK = bank(0, 2), bank(2, 2)
        PF = [bank(4, 2), bank(6, 2)]

        ms, rs = small[:, 0:1], small[:, 1:2]
        eps = small[:, 2:3]
        nmx, sme, rse = small[:, 4:8], small[:, 8:12], small[:, 12:16]
        rr = small[:, 16:36]
        hs, hr = small[:, 36:44], small[:, 44:52]
        fms, frs = small[:, 52:53], small[:, 53:54]

        def col(name, i=0, n=1):
            return cols[:, COL[name] + i:COL[name] + i + n]

        half_ba, half_bx = c_half[:, 0:8], c_half[:, 8:16]
        sp4 = c_half[:, 16:24]
        half_lng, half_lnb = c_half[:, 24:28], c_half[:, 28:32]

        s_cols, s_gm, s_xload = sem("s_cols"), sem("s_gm"), [sem(f"s_xload{i}") for i in range(4)]
        ident_ready, gm_zero, pads_ready = sem("ident_ready"), sem("gm_zero"), sem("pads_ready")
        eps_ready = sem("eps_ready")
        std_ready, rstd_ready, xn_ready = sem("std_ready"), sem("rstd_ready"), sem("xn_ready")
        tr_done, ht_ready = sem("tr_done"), sem("ht_ready")
        w_load = [sem(f"w_load{i}") for i in range(2)]
        item_done, wo_load = sem("item_done"), sem("wo_load")
        job_done, act_took, dve_took = sem("job_done"), sem("act_took"), sem("dve_took")
        xp_ready, tb_ready, xr_ready, gg_ready = (sem(n) for n in
                                                  ("xp_ready", "tb_ready", "xr_ready", "gg_ready"))
        const_half, sp_exp = sem("const_half"), sem("sp_exp")
        gates_ready, q_ready, mult_ready = sem("gates_ready"), sem("q_ready"), sem("mult_ready")
        gates_used, y_ready = sem("gates_used"), sem("y_ready")
        b_done, b_took, b_store = sem("b_done"), sem("b_took"), [sem(f"b_store{i}") for i in range(4)]
        sq_ready, stat_done, yg_ready = sem("sq_ready"), sem("stat_done"), sem("yg_ready")
        conv_ready, mean_done, cen_ready = sem("conv_ready"), sem("mean_done"), sem("cen_ready")
        csq_ready, var_done, sd_ready = sem("csq_ready"), sem("var_done"), sem("sd_ready")
        cn_ready, ct_ready, cs_ready, cg_ready = (sem(n) for n in
                                                  ("cn_ready", "ct_ready", "cs_ready", "cg_ready"))
        c2_ready, srt_ready, rr_ready = sem("c2_ready"), sem("srt_ready"), sem("rr_ready")
        x_again = [sem(f"x_again{i}") for i in range(2)]
        out_done, x1_made = sem("out_done"), sem("x1_made")
        x1_store = [sem(f"x1_store{i}") for i in range(2)]
        act_own, dve_own = sem("act_own"), sem("dve_own")
        wq_load, wp_load, kv_load, wxo_load = (sem(n) for n in
                                               ("wq_load", "wp_load", "kv_load", "wxo_load"))
        x1_load, ss1, rs1, xa_norm, t1_done, h1_ready = (sem(n) for n in
            ("x1_load", "ss1", "rs1", "xa_norm", "t1_done", "h1_ready"))
        q_done, qt_ready, sc_done, mx_ready, p_ready, pn_ready = (sem(n) for n in
            ("q_done", "qt_ready", "sc_done", "mx_ready", "p_ready", "pn_ready"))
        pt_done, pt_ready, o_done, ot_ready, xo_done, x2_ready = (sem(n) for n in
            ("pt_done", "pt_ready", "o_done", "ot_ready", "xo_done", "x2_ready"))
        x2_store, ss2, rs2, xp_norm, t2_done, h2_ready = (sem(n) for n in
            ("x2_store", "ss2", "rs2", "xp_norm", "t2_done", "h2_ready"))
        gp_load, hn_ready, s_done, top_done, ex_in, ex_out = (sem(n) for n in
            ("gp_load", "hn_ready", "s_done", "top_done", "ex_in", "ex_out"))
        idx_ready, idx_taken, h_taken, st_ready = (sem(n) for n in
            ("idx_ready", "idx_taken", "h_taken", "st_ready"))
        row_load = [sem(f"row_load{r}") for r in range(R)]
        dot_ready, act_ready, diag_ready, row_used = (sem(n) for n in
            ("dot_ready", "act_ready", "diag_ready", "row_used"))
        pool_held, sp_held, dve_held = sem("pool_held"), sem("sp_held"), sem("dve_held")
        acc_taken, x2_load, ss3, rs3, y_norm, gf_load, y_ready2, y_store = (sem(n) for n in
            ("acc_taken", "x2_load", "ss3", "rs3", "y_norm", "gf_load", "y_ready2", "y_store"))

        block = ctx.enter_context(nc.Block())

        @block.sync
        def _(sp):
            sp.dma_start(cols[:, :], a["cols"]).then_inc(s_cols, 16)

            def load_x(i):
                if i >= 4:
                    sp.wait_ge(tr_done, i - 3)
                sp.dma_start(xn_p0[i % 4], a["xm"][i * P:(i + 1) * P, :]).then_inc(s_xload[i % 4], 16)

            def load_item(j):
                if j >= 2:
                    sp.wait_ge(item_done, j - 1)
                sp.dma_start(RING[:, (j % 2) * 2 * D:(j % 2 + 1) * 2 * D], a["items"][j])\
                  .then_inc(w_load[j % 2], 16)

            for i in range(4):
                load_x(i)
            sp.wait_ge(gm_zero, 1)
            for e in range(2):
                sp.dma_start(gm[64 * e:64 * e + 64, :, 64 * e:64 * e + 64], a["gates"][e])\
                  .then_inc(s_gm, 16)
            load_item(0)
            load_item(1)
            for i in range(4, NB + MB):
                load_x(i)
            for j in range(2, Z_ITEMS + 2):
                load_item(j)
            sp.wait_ge(item_done, Z_ITEMS)
            sp.dma_start(wo_mix, a["w_out"].rearrange("(k p) n -> p k n", p=P)).then_inc(wo_load, 16)
            for j in range(Z_ITEMS + 2, ITEMS):
                if j == Z_ITEMS + K_ITEMS + V_ITEMS:
                    sp.wait_ge(gates_used, 2 * CH)
                    sp.dma_start(gm, a["subk"]).then_inc(s_gm, 16)
                load_item(j)
            sp.wait_ge(b_took, 48)
            for i in range(4):
                sp.wait_ge(b_store[i], 12 * 16)
            for b in range(2):
                sp.dma_start(XS[:, b * D:(b + 1) * D], a["xm"][b * P:(b + 1) * P, :])\
                  .then_inc(x_again[b], 16)
            sp.wait_ge(rr_ready, 1)
            if not stop_at_x1:
                sp.dma_start(KT, kt_d[0].rearrange("p k n -> p (k n)")).then_inc(kv_load, 16)
                sp.dma_start(VT, v_d[0].rearrange("p k n -> p (k n)")).then_inc(kv_load, 16)
                sp.dma_start(wq, a["w_xq"].rearrange("(k p) n -> p k n", p=P)).then_inc(wq_load, 16)
                sp.dma_start(WP, wp_d.rearrange("p k n -> p (k n)")).then_inc(wp_load, 16)
            for b in range(NB):
                sp.wait_ge(x1_made, b + 1)
                sp.dma_start(x1_d[b * P:(b + 1) * P, :], XS[:, (b % 2) * D:(b % 2 + 1) * D])\
                  .then_inc(x1_store[b % 2], 16)
                if b + 2 < NB:
                    sp.wait_ge(x1_store[b % 2], 16 * (b // 2 + 1))
                    sp.dma_start(XS[:, (b % 2) * D:(b % 2 + 1) * D],
                                 a["xm"][(b + 2) * P:(b + 3) * P, :]).then_inc(x_again[b % 2], 16)
            for i in range(2):
                sp.wait_ge(x1_store[i], 16 * NB // 2)
            if stop_at_x1:
                return
            sp.dma_start(wo, a["w_xo"].rearrange("(k p) n -> p k n", p=P)).then_inc(wxo_load, 16)

            def hold(s, value):
                sp.wait_ge(s, value)
                sp.sem_inc(sp_held, 1)

            def front_loads(b):
                if type(b) is not int or b >= 2:
                    hold(y_ready2, b - 1)
                elif b == 1:
                    hold(idx_ready, 1)
                sp.dma_start(XC, x1_d[ds(b * P, P), :]).then_inc(x1_load, 16)
                if type(b) is not int or b >= 1:
                    hold(h_taken, b)
                sp.dma_start(HN, a["g_peer_row"].partition_broadcast(P)).then_inc(gp_load, 16)
                hold(x2_ready, b + 1)
                sp.dma_start(x2_d[ds(b * P, P), :], XC).then_inc(x2_store, 16)

            def final_loads(b):
                hold(idx_ready, b + 2 if type(b) is not int or b < NB - 1 else NB)
                hold(x2_store, 16 * (b + 2 if type(b) is not int or b < NB - 1 else NB))
                sp.dma_start(XC, x2_d[ds(b * P, P), :]).then_inc(x2_load, 16)
                sp.dma_start(BC, a["g_final_row"].partition_broadcast(P)).then_inc(gf_load, 16)
                hold(y_ready2, b + 1)
                sp.dma_start(a["out"][ds(b * P, P), :], AC).then_inc(y_store, 16)

            front_loads(0)
            front_loads(1)
            final_loads(0)
            sp.wait_ge(pn_ready, 2)
            sp.wait_ge(o_done, 2)
            sp.dma_start(KT, kt_d[1].rearrange("p k n -> p (k n)")).then_inc(kv_load, 16)
            sp.dma_start(VT, v_d[1].rearrange("p k n -> p (k n)")).then_inc(kv_load, 16)
            with sp.Fori(1, NB - 1) as b:
                front_loads(b + 1)
                final_loads(b)
            final_loads(NB - 1)
            sp.wait_ge(y_store, 16 * NB)
            sp.wait_ge(x2_store, 16 * NB)

        @block.gpsimd
        def _(g):
            g.memset(GM, 0.0).then_inc(gm_zero, 1)
            g.memset(ident[:, :], 0.0).then_inc(pool_held, 1)
            g.memset(ones512[:, :], 1.0 / (CH * P)).then_inc(ident_ready, 1)
            g.iota(iota[:, :], pattern=[[1, TOPK]], base=0, channel_multiplier=0,
                   allow_small_or_imprecise_dtypes=True).then_inc(ident_ready, 1)
            g.wait_ge(pool_held, 1)
            g.affine_select(out=ident[:, :], in_=ident[:, :], compare_op=ALU.not_equal, fill=1.0,
                            base=0, pattern=[[-1, P]], channel_multiplier=1).then_inc(ident_ready, 1)
            for c in range(CH):
                g.memset(xp(c, 0, A4), 0.0)
                g.memset(xp(c, A4 + SEQ0, 2), 0.0)
                g.memset(xp(c, B4 + SEQ1, 1), 0.0)
                g.memset(gg(c, SEQ0, 2), 0.0)
                g.memset(ci(c, 0, A31), 0.0)
                g.memset(ci(c, A31 + SEQ0, 15), 0.0)
                g.memset(ci(c, B31 + SEQ1, 15), 0.0).then_inc(pads_ready, 1)

            for n in range(48):
                src = XS[:, (n % 4) * BANK:(n % 4 + 1) * BANK]
                g.wait_ge(b_took, n + 1)
                if n < 8:
                    g.dma_start(kt_d.rearrange("g p k n -> p g k n")[:, :, n, :],
                                src.rearrange("p (g n) -> p g n", g=2)).then_inc(b_store[n % 4], 16)
                elif n < 16:
                    q, grp = (n - 8) // 2, (n - 8) % 2
                    g.dma_start(v_d[grp][:, :, q * 256:(q + 1) * 256],
                                src.rearrange("p (m n) -> p m n", m=2)).then_inc(b_store[n % 4], 16)
                else:
                    i, q = (n - 16) // 4, (n - 16) % 4
                    g.dma_start(wp_d[:, 2 * q:2 * q + 2, i * 256:(i + 1) * 256],
                                src.rearrange("p (m n) -> p m n", m=2)).then_inc(b_store[n % 4], 16)
            if stop_at_x1:
                return

            def hold(s, value):
                g.wait_ge(s, value)
                g.sem_inc(pool_held, 1)

            def gathers(b, group):
                for r in range(R):
                    hold(row_used, (b * (PICKS // R) + group) * R + (r + 1))
                    g.tensor_copy(st[:, r:r + 1], IDXC[:, ds(group * R + r, 1)]).then_inc(st_ready, 1)
                    hold(st_ready, (b * (PICKS // R) + group) * R + (r + 1))
                    g.indirect_dma_start(out=ring[r], out_offset=None, in_=a["uv"],
                                         in_offset=bass.IndirectOffsetOnAxis(ap=st[:, r:r + 1], axis=0))\
                     .then_inc(row_load[r], 16)

            with g.Fori(0, NB) as b:
                hold(idx_ready, b + 1)
                g.tensor_copy(IDXC, IDXN).then_inc(idx_taken, 1)
                hold(idx_taken, b + 1)
                with g.Fori(0, PICKS // R) as group:
                    gathers(b, group)

        @block.scalar
        def _(act):
            own = [0]

            def link(ins):
                own[0] += 1
                ins.then_inc(act_own, 1)
                act.wait_ge(act_own, own[0])

            act.wait_ge(eps_ready, 1)
            for i in range(NB + MB):
                act.wait_ge(s_xload[i % 4], 16 * (i // 4 + 1))
                if i >= 1:
                    act.wait_ge(rstd_ready, i)
                link(act.activation(bank(2 * (i % 2) + 4, 2), xn_p0[i % 4], ACT.Square, accum_out=ms))
                act.activation(rs, ms, ACT.Sqrt, scale=1.0 / D, bias=eps).then_inc(std_ready, 1)
                act.wait_ge(rstd_ready, i + 1)
                act.activation(xn_p0[i % 4], xn_p0[i % 4], ACT.Copy, scale=rs).then_inc(xn_ready, 1)
            act.wait_ge(s_cols, 16)
            link(act.activation(c_half[:, 16:24], col("lam", 0, 8), ACT.Abs))
            act.activation(c_half[:, 16:24], c_half[:, 16:24], ACT.Exp, scale=-1.0).then_inc(sp_exp, 1)
            act.wait_ge(const_half, 1)
            act.wait_ge(pads_ready, CH)

            for n, job in enumerate(JOBS):
                if taker(job) != "act":
                    continue
                src = bank(3 * (n % 2), 3)
                act.wait_ge(job_done, n + 1)
                if job[0] == "z" and job[1] == "x":
                    c = job[2]
                    act.activation(xp(c, A4, SEQ0), src[:, 0:SEQ0], ACT.Copy).then_inc(xp_ready, 1)
                    act.activation(xp(c, B4, SEQ1), src[:, SEQ0:T], ACT.Copy)\
                       .then_inc(act_took, 1)
                elif job[0] == "z" and job[1] == "g":
                    c = job[2]
                    act.activation(gg(c, 0, SEQ0), src[:, 0:SEQ0], ACT.Gelu_apprx_tanh)\
                       .then_inc(gg_ready, 1)
                    act.activation(gg(c, O4, SEQ1), src[:, SEQ0:T], ACT.Gelu_apprx_tanh)\
                       .then_inc(act_took, 1)
                elif job[0] == "z":
                    c = job[2]
                    if c:
                        act.wait_ge(dve_took, c)
                    act.activation(TB[:, 0:T], src[:, 0:T], ACT.Tanh, scale=0.5).then_inc(act_took, 1)
                else:
                    _, kind, d, c = job
                    i = d * CH + c
                    if kind == "a":
                        if c or d:
                            act.wait_ge(gates_used, 2 * c + d)
                        A = AF if d == 0 else AB
                        ins = act.activation(TH[:, 0:L4], src[:, 0:L4], ACT.Tanh, scale=0.5,
                                             bias=half_ba[:, i:i + 1])
                        ins.then_inc(act_took, 1)
                        act.wait_ge(act_took, taken_before(n, "act") + 1)
                        link(act.activation(TH[:, 0:L4], TH[:, 0:L4], ACT.Identity,
                                            scale=sp4[:, i:i + 1], bias=sp4[:, i:i + 1]))
                        link(act.activation(A[:, 0:L4], TH[:, 0:L4], ACT.Exp, scale=-1.0))
                        act.activation(TQ[:, 0:L4], TH[:, 0:L4], ACT.Tanh).then_inc(gates_ready, 1)
                        act.activation(A2[:, 0:L4], A[:, 0:L4], ACT.Square).then_inc(gates_ready, 1)
                    else:
                        act.activation(TX[:, 0:L4], src[:, 0:L4], ACT.Tanh, scale=0.5,
                                       bias=half_bx[:, i:i + 1]).then_inc(act_took, 1)
                        act.wait_ge(q_ready, 2 * c + d + 1)
                        act.activation(A2[:, 0:L4], TQ[:, 0:L4], ACT.Sqrt, scale=0.25)\
                           .then_inc(mult_ready, 1)

            for c in range(CH):
                act.wait_ge(y_ready, c + 1)
                act.wait_ge(gates_used, 2 * CH)
                act.activation(sq_rnn[c][:, 0:L4], gg(c, 0, L4), ACT.Square).then_inc(sq_ready, 1)
                act.wait_ge(sq_ready, c + 1)
                act.activation(gg(c, 0, L4), gg(c, 0, L4), ACT.Copy, scale=col("g_rnn", c))\
                   .then_inc(yg_ready, 1)

            for n in range(48):
                act.wait_ge(b_done, n + 1)
                if n >= 4:
                    act.wait_ge(b_store[n % 4], 16 * (n // 4))
                act.activation(XS[:, (n % 4) * BANK:(n % 4 + 1) * BANK], bank(6 + n % 2), ACT.Copy)\
                   .then_inc(b_took, 1)

            for c in range(CH):
                act.wait_ge(cen_ready, c + 1)
                act.activation(ci(c, 0, L31), xp(c, 0, L31), ACT.Square).then_inc(csq_ready, 1)
            act.wait_ge(var_done, 1)
            act.wait_ge(stat_done, 1)
            act.activation(TH[:, 0:L31], bank(3, 3)[:, 0:L31], ACT.Sqrt, bias=eps).then_inc(sd_ready, 1)
            for c in range(CH):
                act.wait_ge(cn_ready, c + 1)
                act.activation(ci(c, 0, L31), xp(c, 0, L31), ACT.Tanh, scale=half_lng[:, c:c + 1],
                               bias=half_lnb[:, c:c + 1]).then_inc(ct_ready, 1)
            for c in range(CH):
                act.wait_ge(cs_ready, c + 1)
                act.activation(ci(c, 0, L31), xp(c, 0, L31), ACT.Square).then_inc(c2_ready, 1)
                act.wait_ge(c2_ready, c + 1)
                act.activation(xp(c, 0, L31), xp(c, 0, L31), ACT.Copy, scale=hs[:, c:c + 1]).then_inc(cg_ready, 1)
            act.wait_ge(stat_done, 2)
            act.activation(rr[:, 0:NB], bank(7)[:, 0:NB], ACT.Sqrt, bias=eps)\
               .then_inc(srt_ready, 1)
            act.activation(rr[:, NB:2 * NB], bank(7)[:, 16:16 + NB], ACT.Sqrt, scale=0.25,
                           bias=eps).then_inc(srt_ready, 1)
            if stop_at_x1:
                return

            def front_norm(b, load, ssq, rsq, normed, src_ready):
                act.wait_ge(load, src_ready)
                act.activation(PF[1], XC, ACT.Square, accum_out=ms)
                act.drain()
                act.activation(rs, ms, ACT.Sqrt, scale=1.0 / D, bias=eps).then_inc(ssq, 1)
                act.wait_ge(rsq, b + 1)
                act.activation(AC, XC, ACT.Copy, scale=rs).then_inc(normed, 1)

            def picks(b, slot, groups):
                def group(i):
                    for r in range(R):
                        act.wait_ge(dot_ready, (b * PICKS + slot * PER) + i * R + (r + 1))
                        act.activation(acts[:, r:r + 1], dots[:, r:r + 1], ACT.Gelu_apprx_tanh)\
                           .then_inc(act_ready, 1)
                with act.Fori(0, groups) as i:
                    group(i)

            def front(b, walk):
                if type(b) is not int:
                    act.wait_ge(y_store, 16 * b - 16)
                front_norm(b, x1_load, ss1, rs1, xa_norm, 16 * b + 16)
                walk(0)
                walk(1)
                act.wait_ge(q_done, b + 1)
                act.activation(AC, PF[1], ACT.Copy, scale=1.0 / 16).then_inc(qt_ready, 1)
                walk(2)
                act.wait_ge(mx_ready, b + 1)
                for h in range(NH):
                    ins = act.activation(BC[:, h * NMEM:(h + 1) * NMEM], PF[0][:, h * NMEM:(h + 1) * NMEM],
                                         ACT.Exp, bias=nmx[:, h:h + 1], accum_out=sme[:, h:h + 1])
                ins.then_inc(p_ready, 1)
                walk(3)
                act.wait_ge(pt_done, b + 1)
                act.activation(AC, PF[1], ACT.Copy).then_inc(pt_ready, 1)
                act.wait_ge(o_done, b + 1)
                act.activation(BC, PF[0], ACT.Copy).then_inc(ot_ready, 1)
                walk(4)
                walk(5)
                front_norm(b, x2_ready, ss2, rs2, xp_norm, b + 1)
                for s in range(6, 15):
                    walk(s)
                act.wait_ge(ex_in, b + 1)
                act.activation(CV, CV, ACT.Exp).then_inc(ex_out, 1)
                walk(15)

            def final(b):
                act.wait_ge(acc_taken, b + 1)
                act.activation(PF[1], XC, ACT.Square, accum_out=fms)
                act.drain()
                act.activation(frs, fms, ACT.Sqrt, scale=1.0 / D, bias=eps).then_inc(ss3, 1)
                act.wait_ge(rs3, b + 1)
                act.activation(AC, XC, ACT.Copy, scale=frs).then_inc(y_norm, 1)

            front(0, lambda s: None)
            front(1, lambda s: picks(0, s, PER // R))
            final(0)
            with act.Fori(1, NB - 1) as b:
                front(b + 1, lambda s: picks(b, s, PER // R))
                final(b)
            picks(NB - 1, 0, PICKS // R)
            final(NB - 1)

        @block.vector
        def _(v):
            own = [0]

            def link(ins):
                own[0] += 1
                ins.then_inc(dve_own, 1)
                v.wait_ge(dve_own, own[0])

            v.memset(eps, EPS).then_inc(eps_ready, 1)

            def recip_rstd(i):
                v.wait_ge(std_ready, i + 1)
                v.reciprocal(rs, rs).then_inc(rstd_ready, 1)

            def evacuate(i):
                v.wait_ge(tr_done, i + 1)
                dst = hT[:, :, i * P:(i + 1) * P] if i < NB else mT[:, :, (i - NB) * P:(i - NB + 1) * P]
                g = col("g_mix" if i < NB else "g_mem", 0, KD)
                v.tensor_tensor(dst, bank(2 * (i % 2), 2).rearrange("p (k t) -> p k t", k=KD),
                                g.unsqueeze(2).to_broadcast([P, KD, P]), ALU.mult).then_inc(ht_ready, 1)

            v.wait_ge(s_cols, 16)
            for i in range(NB + MB):
                recip_rstd(i)
                if i:
                    evacuate(i - 1)
            evacuate(NB + MB - 1)

            v.tensor_scalar(half_ba, col("ba", 0, 8), 0.5, None, ALU.mult)
            v.tensor_scalar(half_bx, col("bx", 0, 8), 0.5, None, ALU.mult)
            v.tensor_scalar(half_lng, col("ln_g", 0, 4), 0.5, None, ALU.mult)
            v.tensor_scalar(half_lnb, col("ln_b", 0, 4), 0.5, None, ALU.mult)
            v.tensor_scalar(hs[:, 0:4], col("g_conv", 0, 4), 0.5, None, ALU.mult)
            link(v.tensor_scalar(col("conv31_w", 0, TAPS31 * CH), col("conv31_w", 0, TAPS31 * CH), 0.5,
                                 None, ALU.mult))
            e, z, z2, acc = sp4, rr[:, 0:8], rr[:, 8:16], hr
            v.wait_ge(sp_exp, 1)
            link(v.tensor_scalar(z, e, 2.0, None, ALU.add))
            link(v.reciprocal(z, z))
            link(v.tensor_tensor(z, z, e, ALU.mult))
            link(v.tensor_tensor(z2, z, z, ALU.mult))
            link(v.tensor_scalar(acc, z2, 8.0 / 19, 8.0 / 17, ALU.mult, ALU.add))
            for n in (15, 13, 11, 9, 7, 5, 3, 1):
                link(v.tensor_tensor(acc, acc, z2, ALU.mult))
                link(v.tensor_scalar(acc, acc, 8.0 / n, None, ALU.add))
            link(v.tensor_tensor(acc, acc, z, ALU.mult))
            link(v.tensor_scalar(z2, col("lam", 0, 8), -4.0, 0.0, ALU.mult, ALU.max))
            v.tensor_tensor(sp4, acc, z2, ALU.add).then_inc(const_half, 1)

            def conv4(c):
                v.wait_ge(xp_ready, c + 1)
                v.wait_ge(act_took, c + 1)
                if c >= 2:
                    v.wait_ge(job_done, JOBS.index(("gate", "x", 1, c - 2)) + 1)
                w = [col("conv4_w", j * CH + c) for j in range(TAPS4)]
                link(v.tensor_scalar(xr(c, 0, L4), xp(c, 0, L4), w[0], col("conv4_b", c), ALU.mult, ALU.add))
                for j in range(1, TAPS4):
                    ins = v.scalar_tensor_tensor(xr(c, 0, L4), xp(c, j, L4), w[j], xr(c, 0, L4),
                                                 ALU.mult, ALU.add)
                    if j < TAPS4 - 1:
                        link(ins)
                ins.then_inc(xr_ready, 1)

            def glu(c):
                n = JOBS.index(("z", "a", c))
                v.wait_ge(job_done, n + 1)
                v.wait_ge(act_took, taken_before(n, "act"))
                v.wait_ge(pads_ready, CH)
                src = bank(3 * (n % 2), 3)
                v.scalar_tensor_tensor(ci(c, A31, SEQ0), TB[:, 0:SEQ0], 1.0, src[:, 0:SEQ0], ALU.add, ALU.mult)
                v.scalar_tensor_tensor(ci(c, B31, SEQ1), TB[:, SEQ0:T], 1.0, src[:, SEQ0:T], ALU.add,
                                       ALU.mult).then_inc(dve_took, 1)

            def lru(c):
                for d in range(2):
                    n = 2 * c + d
                    A = AF if d == 0 else AB
                    v.wait_ge(gates_ready, 2 * n + 2)
                    v.scalar_tensor_tensor(TQ[:, 0:L4], A2[:, 0:L4], 1.0, TQ[:, 0:L4], ALU.add, ALU.mult)\
                     .then_inc(q_ready, 1)
                    v.wait_ge(act_took, taken_before(JOBS.index(("gate", "x", d, c)), "act") + 1)
                    link(v.scalar_tensor_tensor(TX[:, 0:L4], TX[:, 0:L4], 1.0, xr(c, 0, L4), ALU.add, ALU.mult))
                    v.wait_ge(mult_ready, n + 1)
                    link(v.tensor_tensor(TX[:, 0:L4], TX[:, 0:L4], A2[:, 0:L4], ALU.mult))
                    if d == 0:
                        v.tensor_tensor_scan(TH[:, 0:SEQ0], A[:, 0:SEQ0], TX[:, 0:SEQ0], 0.0, ALU.mult, ALU.add)
                        link(v.tensor_tensor_scan(TH[:, O4:L4], A[:, O4:L4], TX[:, O4:L4], 0.0, ALU.mult, ALU.add))
                        link(v.tensor_copy(A[:, 0:SEQ0], TH[:, 0:SEQ0]))
                        v.tensor_copy(A[:, O4:L4], TH[:, O4:L4]).then_inc(gates_used, 1)
                    else:
                        def back(t, lo, hi):
                            return t[:, lo:hi][:, ::-1]
                        v.tensor_tensor_scan(back(TH, 0, SEQ0), back(A, 0, SEQ0), back(TX, 0, SEQ0), 0.0,
                                             ALU.mult, ALU.add)
                        link(v.tensor_tensor_scan(back(TH, O4, L4), back(A, O4, L4), back(TX, O4, L4), 0.0,
                                                  ALU.mult, ALU.add))
                        for lo, hi in ((0, SEQ0), (O4, L4)):
                            ins = v.tensor_tensor(AF[:, lo:hi], AF[:, lo:hi], TH[:, lo:hi], ALU.add)
                            link(ins)
                        n_g = JOBS.index(("z", "g", c))
                        v.wait_ge(gg_ready, c + 1)
                        v.wait_ge(act_took, taken_before(n_g, "act") + 1)
                        v.tensor_tensor(gg(c, 0, SEQ0), AF[:, 0:SEQ0], gg(c, 0, SEQ0), ALU.mult)
                        link(v.tensor_tensor(gg(c, O4, SEQ1), AF[:, O4:L4], gg(c, O4, SEQ1), ALU.mult))
                        v.sem_inc(gates_used, 1)
                        v.sem_inc(y_ready, 1)

            conv4(0)
            conv4(1)
            for c in range(CH):
                glu(c)
                lru(c)
                if c + 2 < CH:
                    conv4(c + 2)
            for c in range(CH):
                w = [col("conv31_w", j * CH + c) for j in range(TAPS31)]
                link(v.tensor_scalar(xp(c, 0, L31), ci(c, 0, L31), w[0], col("conv31_b", c), ALU.mult, ALU.add))
                for j in range(1, TAPS31):
                    ins = v.scalar_tensor_tensor(xp(c, 0, L31), ci(c, j, L31), w[j], xp(c, 0, L31),
                                                 ALU.mult, ALU.add)
                    if j < TAPS31 - 1:
                        link(ins)
                ins.then_inc(conv_ready, 1)
            v.wait_ge(mean_done, 1)
            for c in range(CH):
                v.tensor_tensor(xp(c, 0, L31), xp(c, 0, L31), bank(0, 3)[:, 0:L31], ALU.subtract)\
                 .then_inc(cen_ready, 1)
            v.wait_ge(sd_ready, 1)
            link(v.reciprocal(TH[:, 0:L31], TH[:, 0:L31]))
            for c in range(CH):
                v.wait_ge(csq_ready, c + 1)
                v.tensor_tensor(xp(c, 0, L31), xp(c, 0, L31), TH[:, 0:L31], ALU.mult).then_inc(cn_ready, 1)
            for c in range(CH):
                v.wait_ge(ct_ready, c + 1)
                link(v.tensor_scalar(xp(c, 0, L31), xp(c, 0, L31), col("ln_g", c), col("ln_b", c),
                                     ALU.mult, ALU.add))
                v.scalar_tensor_tensor(xp(c, 0, L31), ci(c, 0, L31), 1.0, xp(c, 0, L31), ALU.add, ALU.mult)\
                 .then_inc(cs_ready, 1)
            v.wait_ge(srt_ready, 2)
            v.reciprocal(rr, rr).then_inc(rr_ready, 1)
            v.wait_ge(rr_ready, 1)
            for b in range(NB):
                x = XS[:, (b % 2) * D:(b % 2 + 1) * D]
                v.wait_ge(out_done, b + 1)
                v.wait_ge(x_again[b % 2], 16 * (b // 2 + 1))
                link(v.scalar_tensor_tensor(x, bank(4 * (b % 2), 2), rr[:, b:b + 1], x, ALU.mult, ALU.add))
                v.scalar_tensor_tensor(x, bank(4 * (b % 2) + 2, 2), rr[:, NB + b:NB + b + 1], x, ALU.mult,
                                       ALU.add).then_inc(x1_made, 1)
            if stop_at_x1:
                return

            def hold(s, value):
                v.wait_ge(s, value)
                v.sem_inc(dve_held, 1)

            def pick(k, n, group, r):
                v.wait_ge(row_load[r], group * 16 + 16)
                v.scalar_tensor_tensor(out=JUNK, in0=ring[r][:, 0:D], scalar=1.0, in1=HC, op0=ALU.mult,
                                       op1=ALU.mult, accum_out=dots[:, r:r + 1]).then_inc(dot_ready, 1)
                v.wait_ge(act_ready, n + 1)
                v.tensor_scalar(diag[:, r * P:(r + 1) * P], ident[:, :], acts[:, r:r + 1],
                                GATC[:, ds(k, 1)], ALU.mult, ALU.mult).then_inc(diag_ready, 1)

            def picks(b, slot, groups):
                with v.Fori(0, groups) as i:
                    for r in range(R):
                        pick(slot * PER + i * R + r, (b * PICKS + slot * PER) + i * R + r,
                             (b * (PICKS // R) + slot * (PER // R)) + i, r)

            def top16(q):
                src = bank(4 + q)
                sets = [(4 * q + j, src[:, j * NK:(j + 1) * NK], AC[:, j * NK:(j + 1) * NK]) for j in range(4)]
                for m, s, _ in sets:
                    v.max(SV[:, m * 16:m * 16 + 8], s)
                v.drain()
                for m, s, w in sets:
                    v.max_index(SI[:, m * 16:m * 16 + 8], SV[:, m * 16:m * 16 + 8], s)
                    v.match_replace(w, SV[:, m * 16:m * 16 + 8], s, -3e38)
                v.drain()
                for m, _, w in sets:
                    v.max(SV[:, m * 16 + 8:m * 16 + 16], w)
                v.drain()
                for m, _, w in sets:
                    v.max_index(SI[:, m * 16 + 8:m * 16 + 16], SV[:, m * 16 + 8:m * 16 + 16], w)

            def cand_sums():
                v.drain()
                for h in range(PH):
                    v.tensor_tensor(CAND[:, h * 256:(h + 1) * 256].rearrange("p (i j) -> p i j", i=TOPK),
                                    SV[:, h * 32:h * 32 + 16].unsqueeze(2).to_broadcast([P, TOPK, TOPK]),
                                    SV[:, h * 32 + 16:h * 32 + 32].unsqueeze(1).to_broadcast([P, TOPK, TOPK]),
                                    ALU.add)
                v.tensor_copy(SIF, SI)
                v.drain()

            def cand_top(h0, h1):
                hh = [(CAND[:, h * 256:(h + 1) * 256], h * 16) for h in range(h0, h1)]
                for s, o in hh:
                    v.max(CV[:, o:o + 8], s)
                v.drain()
                for s, o in hh:
                    v.max_index(CI16[:, o:o + 8], CV[:, o:o + 8], s)
                v.drain()
                for s, o in hh:
                    v.match_replace(s, CV[:, o:o + 8], s, -3e38)
                v.drain()
                for s, o in hh:
                    v.max(CV[:, o + 8:o + 16], s)
                v.drain()
                for s, o in hh:
                    v.max_index(CI16[:, o + 8:o + 16], CV[:, o + 8:o + 16], s)
                v.drain()

            def pick_index(b):
                cv = CV.rearrange("p (h k) -> p h k", h=PH)
                v.tensor_scalar(IDXN, CI16, 4, None, ALU.logical_shift_right)
                v.tensor_scalar(CI16, CI16, 15, None, ALU.bitwise_and)
                v.drain()
                v.tensor_copy(I0, IDXN)
                v.tensor_copy(I1, CI16)
                v.drain()
                oh = CAND.rearrange("p (k i) -> p k i", i=TOPK)
                oh4 = CAND.rearrange("p (h k i) -> p h k i", h=PH, k=TOPK)
                sif = SIF.rearrange("p (h s i) -> p h s i", h=PH, s=2)
                for side, idx, dst in ((0, I0, E0), (1, I1, I1)):
                    v.tensor_tensor(oh, idx.unsqueeze(2).to_broadcast([P, PICKS, TOPK]),
                                    iota[:, :].unsqueeze(1).to_broadcast([P, PICKS, TOPK]), ALU.is_equal)
                    v.drain()
                    v.tensor_tensor(oh4, oh4, sif[:, :, side, :].unsqueeze(2).to_broadcast([P, PH, TOPK, TOPK]),
                                    ALU.mult)
                    v.drain()
                    v.tensor_reduce(dst, oh, X, ALU.add)
                    v.drain()
                v.scalar_tensor_tensor(IDXN, E0, float(NK), I1, ALU.mult, ALU.add)
                v.drain()
                v.wait_ge(ex_out, b + 1)
                v.tensor_reduce(hs, cv, X, ALU.add)
                v.drain()
                v.reciprocal(hr, hs)
                v.drain()
                v.tensor_tensor(GATN.rearrange("p (h k) -> p h k", h=PH), cv,
                                hr.unsqueeze(2).to_broadcast([P, PH, TOPK]), ALU.mult).then_inc(idx_ready, 1)

            def gate_in(b):
                cv = CV.rearrange("p (h k) -> p h k", h=PH)
                v.tensor_copy(hs, cv[:, :, 0])
                v.drain()
                v.tensor_tensor(cv, cv, hs.unsqueeze(2).to_broadcast([P, PH, TOPK]), ALU.subtract)\
                 .then_inc(ex_in, 1)

            def kt3(t):
                return t.rearrange("p (k t) -> p k t", k=KD)

            def front(b, walk):
                v.wait_ge(ss1, b + 1)
                v.reciprocal(rs, rs).then_inc(rs1, 1)
                v.wait_ge(t1_done, b + 1)
                v.tensor_tensor(kt3(BC), kt3(PF[0]), col("g_xattn", 0, KD).unsqueeze(2).to_broadcast([P, KD, P]),
                                ALU.mult).then_inc(h1_ready, 1)
                walk(0)
                walk(1)
                walk(2)
                v.wait_ge(sc_done, b + 1)
                v.tensor_reduce(nmx, PF[0].rearrange("p (h m) -> p h m", h=NH), X, ALU.max, negate=True)\
                 .then_inc(mx_ready, 1)
                v.wait_ge(p_ready, b + 1)
                v.reciprocal(rse, sme)
                v.drain()
                v.tensor_tensor(BC.rearrange("p (h m) -> p h m", h=NH), BC.rearrange("p (h m) -> p h m", h=NH),
                                rse.unsqueeze(2).to_broadcast([P, NH, NMEM]), ALU.mult).then_inc(pn_ready, 1)
                walk(3)
                walk(4)
                walk(5)
                v.wait_ge(xo_done, b + 1)
                v.tensor_tensor(XC, XC, PF[1], ALU.add).then_inc(x2_ready, 1)
                v.wait_ge(ss2, b + 1)
                v.reciprocal(rs, rs).then_inc(rs2, 1)
                walk(6)
                v.wait_ge(t2_done, b + 1)
                v.tensor_tensor(kt3(BC), kt3(PF[0]), col("g_peer", 0, KD).unsqueeze(2).to_broadcast([P, KD, P]),
                                ALU.mult).then_inc(h2_ready, 1)
                v.wait_ge(gp_load, 16 * b + 16)
                v.wait_ge(xp_norm, b + 1)
                v.tensor_tensor(HN, HN, AC, ALU.mult).then_inc(hn_ready, 1)
                hold(x2_store, 16 * b + 16)
                hold(hn_ready, b + 1)
                walk(7)
                for q in range(4):
                    walk(8 + q)
                    hold(s_done, 4 * b + (q + 1))
                    top16(q)
                cand_sums()
                walk(12)
                cand_top(0, 4)
                walk(13)
                cand_top(4, 8)
                gate_in(b)
                walk(14)
                if type(b) is not int or b >= 1:
                    v.wait_ge(idx_taken, b)
                pick_index(b)
                walk(15)

            def take_over(b):
                v.wait_ge(idx_ready, b + 1)
                v.tensor_copy(HC, HN).then_inc(h_taken, 1)
                v.tensor_copy(GATC, GATN)
                v.drain()

            def final(b):
                v.wait_ge(row_used, (b + 1) * PICKS + R)
                v.wait_ge(x2_load, 16 * b + 16)
                v.tensor_tensor(XC, XC, ACC, ALU.add).then_inc(acc_taken, 1)
                v.wait_ge(ss3, b + 1)
                v.reciprocal(frs, frs).then_inc(rs3, 1)
                v.wait_ge(gf_load, 16 * b + 16)
                v.wait_ge(y_norm, b + 1)
                v.tensor_tensor(AC, AC, BC, ALU.mult).then_inc(y_ready2, 1)

            front(0, lambda s: None)
            take_over(0)
            front(1, lambda s: picks(0, s, PER // R))
            final(0)
            take_over(1)
            with v.Fori(1, NB - 1) as b:
                front(b + 1, lambda s: picks(b, s, PER // R))
                final(b)
                take_over(b + 1)
            picks(NB - 1, 0, PICKS // R)
            final(NB - 1)

        @block.tensor
        def _(t):
            t.wait_ge(ident_ready, 3)
            for i in range(NB + MB):
                t.wait_ge(xn_ready, i + 1)
                if i >= 2:
                    t.wait_ge(ht_ready, i - 1)
                for k in range(KD):
                    ins = t.transpose(ps[:, (i % 2) * 1024 + k * P:(i % 2) * 1024 + (k + 1) * P],
                                      xn_p0[i % 4][:, k * P:(k + 1) * P], ident[:, :])
                ins.then_inc(tr_done, 1)
            t.wait_ge(ht_ready, NB + MB)

            def item(j):
                t.wait_ge(w_load[j % 2], 16 * (j // 2 + 1))
                return RING[:, (j % 2) * 2 * D:(j % 2 + 1) * 2 * D]

            def tiles(total):
                return [(lo, min(BANK, total - lo)) for lo in range(0, total, BANK)]

            t.wait_ge(s_gm, 32)
            zs = 0
            for n, job in enumerate(JOBS):
                if n >= 2:
                    prev = n - 2
                    if taker(JOBS[prev]) == "act":
                        t.wait_ge(act_took, taken_before(prev, "act") + 1)
                    else:
                        t.wait_ge(dve_took, taken_before(prev, "dve") + 1)
                base = 3 * (n % 2) * BANK
                if job[0] == "z":
                    w = item(zs // 2)[:, (zs % 2) * D:(zs % 2 + 1) * D]
                    for lo, size in tiles(T):
                        for k in range(KD):
                            ins = t.matmul(ps[:, base + lo:base + lo + size], w[:, k * P:(k + 1) * P],
                                           hT[:, k, lo:lo + size], start=k == 0, stop=k == KD - 1)
                    ins.then_inc(job_done, 1)
                    zs += 1
                    if zs % 2 == 0:
                        t.wait_ge(job_done, n + 1)
                        t.sem_inc(item_done, 1)
                else:
                    _, kind, d, c = job
                    t.wait_ge(xr_ready, c + 1)
                    m = (0 if kind == "a" else 2 * CH) + d * CH + c
                    for lo, size in tiles(L4):
                        ins = t.matmul(ps[:, base + lo:base + lo + size], gm[:, m, :], xr(c, lo, size),
                                       start=True, stop=True)
                    ins.then_inc(job_done, 1)

            n = 0

            def b_job():
                if n >= 2:
                    t.wait_ge(b_took, n - 1)
                return bank(6 + n % 2)

            for j in range(Z_ITEMS, ITEMS):
                w = item(j)
                if j < Z_ITEMS + K_ITEMS:
                    for m in range(2):
                        o = b_job()
                        for k in range(KD):
                            ins = t.matmul(o, w[:, m * D + k * P:m * D + (k + 1) * P], mT[:, k, :],
                                           start=k == 0, stop=k == KD - 1)
                        ins.then_inc(b_done, 1)
                        n += 1
                elif j < Z_ITEMS + K_ITEMS + V_ITEMS:
                    for grp in range(2):
                        o = b_job()
                        for mb in range(2):
                            for k in range(KD):
                                tok = (2 * grp + mb) * P
                                ins = t.matmul(o[:, mb * 256:(mb + 1) * 256], mT[:, k, tok:tok + P],
                                               w[:, k * 256:(k + 1) * 256], start=k == 0, stop=k == KD - 1)
                        ins.then_inc(b_done, 1)
                        n += 1
                else:
                    i = j - Z_ITEMS - K_ITEMS - V_ITEMS
                    if i == 0:
                        t.wait_ge(gates_used, 2 * CH)
                        t.wait_ge(s_gm, 48)
                    for q in range(4):
                        o = b_job()
                        for dq in range(2):
                            for m in range(2):
                                dd = (2 * q + dq) * P
                                ins = t.matmul(o[:, (2 * dq + m) * P:(2 * dq + m + 1) * P],
                                               w[:, m * D + dd:m * D + dd + P], gm[:, 2 * i + m, :],
                                               start=True, stop=True)
                        ins.then_inc(b_done, 1)
                        n += 1
                t.wait_ge(b_done, n)
                t.sem_inc(item_done, 1)

            t.wait_ge(sq_ready, CH)
            t.wait_ge(b_took, 48)
            for b in range(NB):
                lo = b * P if b < NB0 else O4 + (b - NB0) * P
                for c in range(CH):
                    ins = t.matmul(bank(7)[:, b:b + 1], sq_rnn[c][:, lo:lo + P], ones512[:, 0:1],
                                   start=c == 0, stop=c == CH - 1)
            ins.then_inc(stat_done, 1)
            t.wait_ge(conv_ready, CH)
            t.wait_ge(act_took, taken_before(len(JOBS), "act"))
            for lo, size in tiles(L31):
                for c in range(CH):
                    ins = t.matmul(ps[:, lo:lo + size], ones512[:, :], xp(c, lo, size),
                                   start=c == 0, stop=c == CH - 1)
            ins.then_inc(mean_done, 1)
            t.wait_ge(csq_ready, CH)
            for lo, size in tiles(L31):
                for c in range(CH):
                    ins = t.matmul(ps[:, 3 * BANK + lo:3 * BANK + lo + size], ones512[:, :], ci(c, lo, size),
                                   start=c == 0, stop=c == CH - 1)
            ins.then_inc(var_done, 1)
            t.wait_ge(c2_ready, CH)
            for b in range(NB):
                lo = b * P if b < NB0 else O31 + (b - NB0) * P
                for c in range(CH):
                    ins = t.matmul(bank(7)[:, 16 + b:17 + b], ci(c, lo, P), ones512[:, 0:1],
                                   start=c == 0, stop=c == CH - 1)
            ins.then_inc(stat_done, 1)
            t.wait_ge(wo_load, 16)
            t.wait_ge(yg_ready, CH)
            t.wait_ge(cg_ready, CH)
            t.wait_ge(srt_ready, 2)
            for b in range(NB):
                if b >= 2:
                    t.wait_ge(x1_made, b - 1)
                lo4 = b * P if b < NB0 else O4 + (b - NB0) * P
                lo31 = b * P if b < NB0 else O31 + (b - NB0) * P
                for grp in range(2):
                    for half in range(2):
                        o = bank(4 * (b % 2) + 2 * grp + half)
                        for c in range(CH):
                            lhs = gg(c, lo4, P) if grp == 0 else xp(c, lo31, P)
                            ins = t.matmul(o, lhs, wo_mix[:, grp * CH + c, half * BANK:(half + 1) * BANK],
                                           start=c == 0, stop=c == CH - 1)
                ins.then_inc(out_done, 1)
            if stop_at_x1:
                return

            t.wait_ge(x1_made, NB)
            t.sem_inc(row_used, R)

            def pick(n, r, start, stop):
                t.wait_ge(diag_ready, n + 1)
                for half in range(2):
                    ins = t.matmul(ACC[:, half * BANK:(half + 1) * BANK], diag[:, r * P:(r + 1) * P],
                                   ring[r][:, D + half * BANK:D + (half + 1) * BANK], start=start, stop=stop)
                ins.then_inc(row_used, 1)

            def group(b, g, start=False, stop=False):
                for r in range(R):
                    pick(b * PICKS + g * R + r, r, start and r == 0, stop and r == R - 1)

            def picks(b, slot):
                g0, n = slot * (PER // R), PER // R
                if slot == 0:
                    if type(b) is not int or b:
                        t.wait_ge(acc_taken, b)
                    group(b, 0, start=True)
                    g0, n = 1, n - 1
                if slot == SLOTS - 1:
                    n -= 1
                with t.Fori(0, n) as i:
                    group(b, g0 + i)
                if slot == SLOTS - 1:
                    group(b, PICKS // R - 1, stop=True)

            def transposes(dst, src):
                for k in range(KD):
                    ins = t.transpose(dst[:, k * P:(k + 1) * P], src[:, k * P:(k + 1) * P], ident[:, :])
                return ins

            def front(b, walk):
                t.wait_ge(xa_norm, b + 1)
                transposes(PF[0], AC).then_inc(t1_done, 1)
                walk(0)
                t.wait_ge(h1_ready, b + 1)
                if type(b) is int and b == 0:
                    t.wait_ge(wq_load, 16)
                for m in range(KD):
                    for k in range(KD):
                        ins = t.matmul(PF[1][:, m * P:(m + 1) * P], wq[:, k, m * P:(m + 1) * P],
                                       BC[:, k * P:(k + 1) * P], start=k == 0, stop=k == KD - 1)
                    if m == KD // 2 - 1:
                        walk(1)
                ins.then_inc(q_done, 1)
                walk(2)
                t.wait_ge(qt_ready, b + 1)
                if type(b) is int and b < 1:
                    t.wait_ge(kv_load, 32)
                if type(b) is not int:
                    t.wait_ge(kv_load, 64)
                for h in range(NH):
                    for j in range(2):
                        k = 2 * h + j
                        ins = t.matmul(PF[0][:, h * NMEM:(h + 1) * NMEM], AC[:, k * P:(k + 1) * P],
                                       kt[:, k, :], start=j == 0, stop=j == 1)
                ins.then_inc(sc_done, 1)
                walk(3)
                t.wait_ge(pn_ready, b + 1)
                transposes(PF[1], BC).then_inc(pt_done, 1)
                t.wait_ge(pt_ready, b + 1)
                for k in range(KD):
                    for j in range(2):
                        ins = t.matmul(PF[0][:, k * P:(k + 1) * P], vt[:, j, k * P:(k + 1) * P],
                                       AC[:, (2 * (k // 2) + j) * P:(2 * (k // 2) + j + 1) * P],
                                       start=j == 0, stop=j == 1)
                ins.then_inc(o_done, 1)
                walk(4)
                t.wait_ge(ot_ready, b + 1)
                if type(b) is int and b == 0:
                    t.wait_ge(wxo_load, 16)
                for half in range(2):
                    for k in range(KD):
                        ins = t.matmul(PF[1][:, half * BANK:(half + 1) * BANK], BC[:, k * P:(k + 1) * P],
                                       wo[:, k, half * BANK:(half + 1) * BANK], start=k == 0, stop=k == KD - 1)
                    if half == 0:
                        walk(5)
                ins.then_inc(xo_done, 1)
                walk(6)
                t.wait_ge(xp_norm, b + 1)
                transposes(PF[0], AC).then_inc(t2_done, 1)
                walk(7)
                t.wait_ge(h2_ready, b + 1)
                if type(b) is int and b == 0:
                    t.wait_ge(wp_load, 16)
                for q in range(4):
                    for k in range(KD):
                        ins = t.matmul(bank(4 + q), BC[:, k * P:(k + 1) * P], wp[:, k, q * BANK:(q + 1) * BANK],
                                       start=k == 0, stop=k == KD - 1)
                    ins.then_inc(s_done, 1)
                    walk(8 + q)
                for s in range(12, 16):
                    walk(s)

            front(0, lambda s: None)
            front(1, lambda s: picks(0, s))
            with t.Fori(1, NB - 1) as b:
                front(b + 1, lambda s: picks(b, s))
            t.wait_ge(acc_taken, NB - 1)
            group(NB - 1, 0, start=True)
            with t.Fori(1, PICKS // R - 1) as g:
                group(NB - 1, g)
            group(NB - 1, PICKS // R - 1, stop=True)


def kernel(**inputs):
    import numpy as np
    import concourse.bacc as bacc
    from concourse.bass_utils import run_bass_kernel_spmd as run
    stop_at_x1 = False

    x = {k: np.asarray(v) for k, v in inputs.items()}
    nc = bacc.Bacc("TRN2", target_bir_lowering=False, num_devices=1)

    def channels(w):
        return w.reshape(-1, P).T

    cols = np.concatenate([channels(x[k][0]) for k in (
        "g_mix", "g_mem", "g_xattn", "g_peer", "conv4_w", "conv4_b", "lru_ba", "lru_bx", "lru_lam",
        "conv31_w", "conv31_b", "conv_ln_g", "conv_ln_b", "g_out_rnn", "g_out_conv")], axis=1)

    def stationary(w):
        return w.reshape(KD, P, -1, P).transpose(2, 1, 0, 3).reshape(-1, P, D)

    w_in = stationary(x["w_in"][0])[[BASE[k] + c for k, c in CHUNKS]]
    w_k = stationary(x["w_xkv"][0][:, :D])
    w_v = x["w_xkv"][0][:, D:].reshape(KD, P, 4, 256).transpose(2, 1, 0, 3).reshape(4, P, 2 * D)
    w_pq = x["w_pq"][0].T.reshape(2 * PH, P, D)

    def paired(w):
        return w.reshape(-1, 2, P, D).transpose(0, 2, 1, 3).reshape(-1, P, 2 * D)

    items = np.concatenate([paired(w_in), paired(w_k), w_v, paired(w_pq)])
    gates = np.stack([x["lru_wa"][0], x["lru_wx"][0]]).reshape(2, 2, CH, 2, 64, 64)\
        .transpose(3, 4, 0, 1, 2, 5).reshape(2, 64, 16, 64)
    arrays = {
        "xm": np.concatenate([x["x_prompt"][0], x["x_sample"][0], x["mem_prompt"][0], x["mem_sample"][0]]),
        "cols": cols, "items": items, "gates": gates,
        "subk": x["peer_sub_keys"][0].reshape(2 * PH, NK, P).transpose(2, 0, 1),
        "w_out": x["w_out"][0], "w_xq": x["w_xq"][0], "w_xo": x["w_xo"][0],
        "g_peer_row": x["g_peer"][0], "g_final_row": x["g_final"],
        "uv": np.concatenate([x["peer_u"][0], x["peer_v"][0]], axis=1),
    }
    arrays = {f"in_{k}": np.ascontiguousarray(v) for k, v in arrays.items()}
    aps = {k[3:]: nc.dram_tensor(k, v.shape, mybir.dt.from_np(v.dtype), kind="ExternalInput").ap()
           for k, v in arrays.items()}
    aps["out"] = nc.dram_tensor("out_0", (T, D), mybir.dt.float32, kind="ExternalOutput").ap()
    build(nc, aps, stop_at_x1)
    y = run(nc, [arrays], core_ids=[0]).results[0]["out_0"]
    return y[None, :SEQ0], y[None, SEQ0:]
```

```python
import concourse.bass as bass
from concourse import mybir
from contextlib import ExitStack

P = 128
D = 1024
KD = D // P
SEQ0, SEQ1 = 256, 1024
T = SEQ0 + SEQ1
NB = T // P
NB0 = SEQ0 // P
NMEM = 256
MB = 2 * NMEM // P
CH = 4
TAPS4, TAPS31 = 4, 31
NH = 4
PH = 8
NK = 128
TOPK = 16
PICKS = PH * TOPK
EPS = 1e-6
BANK = 512

A4, B4 = 2, 2 + SEQ0 + 2
L4 = SEQ0 + 2 + SEQ1
O4 = SEQ0 + 2
A31, B31 = 15, 15 + SEQ0 + 15
L31 = SEQ0 + 15 + SEQ1
O31 = SEQ0 + 15
PITCH = L31 + 30
TP = L31 + 1

COLS = [("g_mix", KD), ("g_mem", KD), ("g_xattn", KD), ("g_peer", KD), ("conv4_w", TAPS4 * CH),
        ("conv4_b", CH), ("ba", 2 * CH), ("bx", 2 * CH), ("lam", 2 * CH), ("conv31_w", TAPS31 * CH),
        ("conv31_b", CH), ("ln_g", CH), ("ln_b", CH), ("g_rnn", CH), ("g_conv", CH)]
COL = {}
NCOL = 0
for _n, _w in COLS:
    COL[_n] = NCOL
    NCOL += _w

CHUNKS = [("x", 0), ("x", 1), ("x", 2), ("x", 3), ("g", 0), ("b", 0), ("a", 0), ("g", 1),
          ("b", 1), ("a", 1), ("g", 2), ("b", 2), ("a", 2), ("g", 3), ("b", 3), ("a", 3)]
BASE = {"x": 0, "g": CH, "a": 2 * CH, "b": 3 * CH}
Z_ITEMS = 8
B_ITEMS = ["k"] * 4 + ["qk"] * 4 + ["v"] * 4 + ["vo"] * 4 + ["w"] * 8
ITEMS = Z_ITEMS + len(B_ITEMS)
W_FIRST = Z_ITEMS + B_ITEMS.index("w")
B_JOBS = [(kind, i, q) for kind, n, per in (("k", 4, 2), ("qk", 4, 8), ("v", 4, 2), ("vo", 4, 8), ("w", 8, 4))
          for i in range(n) for q in range(per)]
STAGED = [n for n, job in enumerate(B_JOBS) if job[0] in ("qk", "vo", "w")]
AT_RNN, AT_MEAN, AT_VAR = 8, 52, 58

JOBS = []
for _kind, _c in CHUNKS:
    JOBS.append(("z", _kind, _c))
    if _kind in "ba":
        JOBS += [("gate", w, int(_kind == "a"), _c) for w in "ax"]

R = 6
GROUPS = PICKS // R
TAIL = (2, 3)
assert GROUPS * R + len(TAIL) == PICKS
USES = [GROUPS + (r in TAIL) for r in range(R)]


MIX_TURN = {1: 0, 2: 4, 3: 5, 4: 6, 5: 7, 6: 8, 7: 10, 8: 11, 9: 12}


def taker(job):
    return "dve" if job[:2] == ("z", "a") else "act"


def taken_before(n, engine):
    return sum(taker(j) == engine for j in JOBS[:n])


def build(nc, a, stop_at_x1=False):
    f32, u32 = mybir.dt.float32, mybir.dt.uint32
    ALU, ACT = mybir.AluOpType, mybir.ActivationFunctionType
    X = mybir.AxisListType.X
    ds = bass.ds

    qk_d = nc.dram_tensor("qk_scratch", (2, P, KD, NH * NMEM), f32).ap()
    vo_d = nc.dram_tensor("vo_scratch", (2, P, KD, D), f32).ap()
    wp_d = nc.dram_tensor("wp_scratch", (P, KD, 2 * PH * NK), f32).ap()
    x1_d = a["out"] if stop_at_x1 else nc.dram_tensor("x1_scratch", (T, D), f32).ap()
    x2_d = nc.dram_tensor("x2_scratch", (T, D), f32).ap()

    ctx = ExitStack()
    with ctx:
        def sb(name, cols, dt=f32):
            return ctx.enter_context(nc.sbuf_tensor(name, [P, cols], dt))

        def sem(name):
            return ctx.enter_context(nc.semaphore(name))

        cols = sb("cols", NCOL)
        c_half = sb("c_half", 8 * CH)
        ident, ones512 = sb("ident", P), sb("ones512", P)
        small = sb("small", 64)
        arena = sb("arena", 51444)
        ps = ctx.enter_context(nc.psum_tensor("ps", [P, 8 * BANK], f32))
        at = [0]

        def piece(words, dt=f32):
            s = arena[:, at[0]:at[0] + words]
            at[0] += words
            return s if dt == f32 else s.bitcast(dt)

        HT = piece(KD * T)
        XP = piece(CH * PITCH)
        GG = piece(CH * TP)
        XS = piece(2 * D)
        zone_d = at[0]
        CI = piece(CH * PITCH)
        kv_at = at[0]
        AF, AB = piece(TP), piece(TP)
        XR = piece(2 * TP)
        TH, TQ, A2, TX = (piece(TP) for _ in range(4))
        MT = piece(KD * MB * P)
        RING = piece(2 * 2 * D)
        GM = piece(16 * P)
        TB = piece(TP)
        hT = HT.rearrange("p (k t) -> p k t", k=KD)
        mT = MT.rearrange("p (k t) -> p k t", k=KD)
        wo_mix = HT[:, 0:KD * D].rearrange("p (k n) -> p k n", k=KD)
        gm = GM.rearrange("p (m n) -> p m n", m=16)
        xn_p0 = [XS[:, 0:D], XS[:, D:2 * D], TH[:, 0:D], TQ[:, 0:D]]
        sq_rnn = [TH, TQ, A2, TX]
        kvT = arena[:, kv_at:kv_at + KD * 2 * NMEM].rearrange("p (k n) -> p k n", k=KD)

        def xp(c, lo, n):
            return XP[:, c * PITCH + lo:c * PITCH + lo + n]

        def ci(c, lo, n):
            return CI[:, c * PITCH + lo:c * PITCH + lo + n]

        def gg(c, lo, n):
            return GG[:, c * TP + lo:c * TP + lo + n]

        def xr(c, lo, n):
            return XR[:, (c % 2) * TP + lo:(c % 2) * TP + lo + n]

        at[0] = 0
        WPB = piece(KD * D)
        GR = piece(R * 2 * D)
        HC = piece(D)
        CI16 = piece(PICKS, u32)
        IDXN, IDXC, GATN, GATC = piece(PICKS, u32), piece(PICKS, u32), piece(PICKS), piece(PICKS)
        assert at[0] <= zone_d
        at[0] = zone_d
        QK = piece(KD * D)
        VO = piece(KD * D)
        WPA = piece(KD * D)
        HN, XC, AC, BC = (piece(D) for _ in range(4))
        assert at[0] <= 51444
        SI = sb("SI", 2 * PH * TOPK, u32)[:, :]
        diag = sb("diag", R * P)
        iota = sb("iota", TOPK)
        st = sb("st", R, u32)
        dots, acts = sb("dots", R), sb("acts", R)
        ring = [GR[:, r * 2 * D:(r + 1) * 2 * D] for r in range(R)]
        qk = QK.rearrange("p (k n) -> p k n", k=KD)
        vo = VO.rearrange("p (k n) -> p k n", k=KD)
        wp = [w.rearrange("p (k n) -> p k n", k=KD) for w in (WPA, WPB)]
        SV, SIF = XC[:, 0:256], XC[:, 256:512]
        CV, I0, I1, E0 = (XC[:, 512 + i * 128:640 + i * 128] for i in range(4))
        CAND = AC[:, 2 * TOPK * TOPK:]
        ONEHOT = arena[:, at[0] - 2 * D:at[0]]

        def bank(b, n=1):
            return ps[:, b * BANK:(b + n) * BANK]

        ACC, JUNK = bank(0, 2), bank(2, 2)
        PF = [bank(4, 2), bank(6, 2)]

        ms, rs = small[:, 0:1], small[:, 1:2]
        eps = small[:, 2:3]
        nmx, sme, rse = small[:, 4:8], small[:, 8:12], small[:, 12:16]
        rr = small[:, 16:36]
        hs, hr = small[:, 36:44], small[:, 44:52]
        fms, frs = small[:, 52:53], small[:, 53:54]

        def col(name, i=0, n=1):
            return cols[:, COL[name] + i:COL[name] + i + n]

        half_ba, half_bx = c_half[:, 0:8], c_half[:, 8:16]
        sp4 = c_half[:, 16:24]
        half_lng, half_lnb = c_half[:, 24:28], c_half[:, 28:32]

        s_cols, s_gm, s_xload = sem("s_cols"), sem("s_gm"), [sem(f"s_xload{i}") for i in range(4)]
        ident_ready, gm_zero, pads_ready = sem("ident_ready"), sem("gm_zero"), sem("pads_ready")
        eps_ready = sem("eps_ready")
        std_ready, rstd_ready, xn_ready = sem("std_ready"), sem("rstd_ready"), sem("xn_ready")
        tr_done, ht_ready = sem("tr_done"), sem("ht_ready")
        w_load = [sem(f"w_load{i}") for i in range(2)]
        item_done, wo_load = sem("item_done"), sem("wo_load")
        job_done, act_took, dve_took = sem("job_done"), sem("act_took"), sem("dve_took")
        xp_ready, tb_ready, xr_ready, gg_ready = (sem(n) for n in
                                                  ("xp_ready", "tb_ready", "xr_ready", "gg_ready"))
        const_half, sp_exp = sem("const_half"), sem("sp_exp")
        gates_ready, q_ready, mult_ready = sem("gates_ready"), sem("q_ready"), sem("mult_ready")
        gates_used, y_ready = sem("gates_used"), sem("y_ready")
        b_done, b_took, b_store = sem("b_done"), sem("b_took"), [sem(f"b_store{i}") for i in range(4)]
        sq_ready, stat_done, yg_ready = sem("sq_ready"), sem("stat_done"), sem("yg_ready")
        conv_ready, mean_done, cen_ready = sem("conv_ready"), sem("mean_done"), sem("cen_ready")
        csq_ready, var_done, sd_ready = sem("csq_ready"), sem("var_done"), sem("sd_ready")
        cn_ready, ct_ready, cs_ready, cg_ready = (sem(n) for n in
                                                  ("cn_ready", "ct_ready", "cs_ready", "cg_ready"))
        c2_ready, srt_ready, rr_ready = sem("c2_ready"), sem("srt_ready"), sem("rr_ready")
        x_again = [sem(f"x_again{i}") for i in range(2)]
        out_done, x1_made = sem("out_done"), sem("x1_made")
        x1_store = [sem(f"x1_store{i}") for i in range(2)]
        act_own, dve_own = sem("act_own"), sem("dve_own")
        qk_load, vo_load, wpa_load, wpb_load = (sem(n) for n in
                                                ("qk_load", "vo_load", "wpa_load", "wpb_load"))
        kv_made, out_took = sem("kv_made"), sem("out_took")
        x1_load, ss1, rs1, xa_norm, t1_done, h1_ready = (sem(n) for n in
            ("x1_load", "ss1", "rs1", "xa_norm", "t1_done", "h1_ready"))
        sc_done, mx_ready, p_ready, pn_ready = (sem(n) for n in
            ("sc_done", "mx_ready", "p_ready", "pn_ready"))
        pt_done, pt_ready, xo_done, x2_ready = (sem(n) for n in
            ("pt_done", "pt_ready", "xo_done", "x2_ready"))
        x2_store, ss2, rs2, xp_norm, t2_done, h2_ready = (sem(n) for n in
            ("x2_store", "ss2", "rs2", "xp_norm", "t2_done", "h2_ready"))
        gp_load, hn_ready, s_done, top_done, ex_in, ex_out = (sem(n) for n in
            ("gp_load", "hn_ready", "s_done", "top_done", "ex_in", "ex_out"))
        idx_ready, idx_taken, h_taken, st_ready = (sem(n) for n in
            ("idx_ready", "idx_taken", "h_taken", "st_ready"))
        row_load = [sem(f"row_load{r}") for r in range(R)]
        dot_ready, act_ready, diag_ready, row_used = (sem(n) for n in
            ("dot_ready", "act_ready", "diag_ready", "row_used"))
        pool_held, sp_held, dve_held = sem("pool_held"), sem("sp_held"), sem("dve_held")
        acc_taken, x2_load, ss3, rs3, y_norm, gf_load, y_ready2, y_store = (sem(n) for n in
            ("acc_taken", "x2_load", "ss3", "rs3", "y_norm", "gf_load", "y_ready2", "y_store"))

        block = ctx.enter_context(nc.Block())

        @block.sync
        def _(sp):
            sp.dma_start(cols[:, :], a["cols"]).then_inc(s_cols, 16)

            def load_x(i):
                if i >= 4:
                    sp.wait_ge(tr_done, i - 3)
                sp.dma_start(xn_p0[i % 4], a["xm"][i * P:(i + 1) * P, :]).then_inc(s_xload[i % 4], 16)

            def load_item(j):
                if j >= 2:
                    sp.wait_ge(item_done, j - 1)
                sp.dma_start(RING[:, (j % 2) * 2 * D:(j % 2 + 1) * 2 * D], a["items"][j])\
                  .then_inc(w_load[j % 2], 16)

            for i in range(4):
                load_x(i)
            sp.wait_ge(gm_zero, 1)
            for e in range(2):
                sp.dma_start(gm[64 * e:64 * e + 64, :, 64 * e:64 * e + 64], a["gates"][e])\
                  .then_inc(s_gm, 16)
            load_item(0)
            load_item(1)
            for i in range(4, NB + MB):
                load_x(i)
            for j in range(2, Z_ITEMS + 2):
                load_item(j)
            sp.wait_ge(item_done, Z_ITEMS)
            sp.dma_start(wo_mix, a["w_out"].rearrange("(k p) n -> p k n", p=P)).then_inc(wo_load, 16)
            for j in range(Z_ITEMS + 2, ITEMS):
                if j == W_FIRST:
                    sp.wait_ge(gates_used, 2 * CH)
                    sp.dma_start(gm, a["subk"]).then_inc(s_gm, 16)
                load_item(j)
            sp.wait_ge(rr_ready, 1)
            for i in range(4):
                sp.wait_ge(b_store[i], 16 * len(STAGED) // 4)
            if stop_at_x1:
                return

            def flat(x):
                return x.rearrange("p k n -> p (k n)")

            sp.dma_start(QK, flat(qk_d[0])).then_inc(qk_load, 16)

            def hold(s, value):
                sp.wait_ge(s, value)
                sp.sem_inc(sp_held, 1)

            def front_loads(b):
                if type(b) is not int:
                    hold(y_ready2, b - 1)
                elif b == 1:
                    hold(idx_ready, 1)
                sp.dma_start(XC, x1_d[ds(b * P, P), :]).then_inc(x1_load, 16)
                if type(b) is not int or b >= 1:
                    hold(h_taken, b)
                sp.dma_start(HN, a["g_peer_row"].partition_broadcast(P)).then_inc(gp_load, 16)

            def store_x2(b):
                hold(x2_ready, b + 1)
                sp.dma_start(x2_d[ds(b * P, P), :], XC).then_inc(x2_store, 16)

            def final_loads(b, fronts):
                hold(idx_ready, fronts)
                hold(x2_store, 16 * fronts)
                sp.dma_start(XC, x2_d[ds(b * P, P), :]).then_inc(x2_load, 16)
                sp.dma_start(BC, a["g_final_row"].partition_broadcast(P)).then_inc(gf_load, 16)

            def store_y(b):
                hold(y_ready2, b + 1)
                sp.dma_start(a["out"][ds(b * P, P), :], AC).then_inc(y_store, 16)

            sp.wait_ge(x1_store[0], 16)
            front_loads(0)
            sp.dma_start(VO, flat(vo_d[0])).then_inc(vo_load, 16)
            sp.dma_start(wp[0], wp_d[:, :, 0:D]).then_inc(wpa_load, 16)
            store_x2(0)
            for i in range(2):
                sp.wait_ge(x1_store[i], 16 * NB // 2)
            sp.dma_start(wp[1], wp_d[:, :, D:2 * D]).then_inc(wpb_load, 16)
            front_loads(1)
            store_x2(1)
            sp.wait_ge(xo_done, 2)
            sp.dma_start(QK, flat(qk_d[1])).then_inc(qk_load, 16)
            sp.dma_start(VO, flat(vo_d[1])).then_inc(vo_load, 16)
            final_loads(0, 2)
            with sp.Fori(1, NB - 1) as b:
                store_y(b - 1)
                front_loads(b + 1)
                store_x2(b + 1)
                final_loads(b, b + 2)
            store_y(NB - 2)
            sp.wait_ge(y_store, 16 * (NB - 1))
            final_loads(NB - 1, NB)
            store_y(NB - 1)
            sp.wait_ge(y_store, 16 * NB)
            sp.wait_ge(x2_store, 16 * NB)

        @block.gpsimd
        def _(g):
            g.memset(GM, 0.0).then_inc(gm_zero, 1)
            g.memset(ident[:, :], 0.0).then_inc(pool_held, 1)
            g.memset(ones512[:, :], 1.0 / (CH * P)).then_inc(ident_ready, 1)
            g.iota(iota[:, :], pattern=[[1, TOPK]], base=0, channel_multiplier=0,
                   allow_small_or_imprecise_dtypes=True).then_inc(ident_ready, 1)
            g.wait_ge(pool_held, 1)
            g.affine_select(out=ident[:, :], in_=ident[:, :], compare_op=ALU.not_equal, fill=1.0,
                            base=0, pattern=[[-1, P]], channel_multiplier=1).then_inc(ident_ready, 1)
            for c in range(CH):
                g.memset(xp(c, 0, A4), 0.0)
                g.memset(xp(c, A4 + SEQ0, 2), 0.0)
                g.memset(xp(c, B4 + SEQ1, 1), 0.0)
                g.memset(gg(c, SEQ0, 2), 0.0)
                g.memset(ci(c, 0, A31), 0.0)
                g.memset(ci(c, A31 + SEQ0, 15), 0.0)
                g.memset(ci(c, B31 + SEQ1, 15), 0.0).then_inc(pads_ready, 1)

            for m, n in enumerate(STAGED):
                kind, i, q = B_JOBS[n]
                src = XS[:, (m % 4) * BANK:(m % 4 + 1) * BANK]
                two = src.rearrange("p (m n) -> p m n", m=2)
                g.wait_ge(b_took, n + 1)
                if kind == "qk":
                    dst, src = qk_d.rearrange("g p k n -> p g k n")[:, :, q, i * NMEM:(i + 1) * NMEM], two
                elif kind == "vo":
                    dst = vo_d[q // 4][:, 2 * i + q // 2 % 2, (q % 2) * BANK:(q % 2 + 1) * BANK]
                else:
                    dst, src = wp_d[:, 2 * q:2 * q + 2, i * 256:(i + 1) * 256], two
                g.dma_start(dst, src).then_inc(b_store[m % 4], 16)
            for i in range(4):
                g.wait_ge(b_store[i], 16 * len(STAGED) // 4)

            def x_tile(b):
                return XS[:, (b % 2) * D:(b % 2 + 1) * D]

            for b in range(2):
                g.dma_start(x_tile(b), a["xm"][b * P:(b + 1) * P, :]).then_inc(x_again[b], 16)
            for b in range(NB):
                g.wait_ge(x1_made, b + 1)
                g.dma_start(x1_d[b * P:(b + 1) * P, :], x_tile(b)).then_inc(x1_store[b % 2], 16)
                if b + 2 < NB:
                    g.wait_ge(x1_store[b % 2], 16 * (b // 2 + 1))
                    g.dma_start(x_tile(b), a["xm"][(b + 2) * P:(b + 3) * P, :]).then_inc(x_again[b % 2], 16)
            for i in range(2):
                g.wait_ge(x1_store[i], 16 * NB // 2)
            if stop_at_x1:
                return

            def hold(s, value):
                g.wait_ge(s, value)
                g.sem_inc(pool_held, 1)

            def gather(b, group, r, tail=False):
                k = group * R + (r - TAIL[0] if tail else r)
                hold(row_used, b * PICKS + k + 1 + (2 if tail or (type(group) is int and r in TAIL) else 0))
                g.tensor_copy(st[:, r:r + 1], IDXC[:, ds(k, 1)]).then_inc(st_ready, 1)
                hold(st_ready, b * PICKS + k + 1)
                g.indirect_dma_start(out=ring[r], out_offset=None, in_=a["uv"],
                                     in_offset=bass.IndirectOffsetOnAxis(ap=st[:, r:r + 1], axis=0))\
                 .then_inc(row_load[r], 16)

            with g.Fori(0, NB) as b:
                hold(idx_ready, b + 1)
                g.tensor_copy(IDXC, IDXN).then_inc(idx_taken, 1)
                hold(idx_taken, b + 1)
                for r in range(R):
                    gather(b, 0, r)
                with g.Fori(1, GROUPS) as group:
                    for r in range(R):
                        gather(b, group, r)
                for r in TAIL:
                    gather(b, GROUPS, r, tail=True)

        @block.scalar
        def _(act):
            own = [0]

            def link(ins):
                own[0] += 1
                ins.then_inc(act_own, 1)
                act.wait_ge(act_own, own[0])

            act.wait_ge(eps_ready, 1)
            for i in range(NB + MB):
                act.wait_ge(s_xload[i % 4], 16 * (i // 4 + 1))
                if i >= 1:
                    act.wait_ge(rstd_ready, i)
                link(act.activation(bank(2 * (i % 2) + 4, 2), xn_p0[i % 4], ACT.Square, accum_out=ms))
                act.activation(rs, ms, ACT.Sqrt, scale=1.0 / D, bias=eps).then_inc(std_ready, 1)
                act.wait_ge(rstd_ready, i + 1)
                act.activation(xn_p0[i % 4], xn_p0[i % 4], ACT.Copy, scale=rs).then_inc(xn_ready, 1)
            act.wait_ge(s_cols, 16)
            link(act.activation(c_half[:, 16:24], col("lam", 0, 8), ACT.Abs))
            act.activation(c_half[:, 16:24], c_half[:, 16:24], ACT.Exp, scale=-1.0).then_inc(sp_exp, 1)
            act.wait_ge(const_half, 1)
            act.wait_ge(pads_ready, CH)

            for n, job in enumerate(JOBS):
                if taker(job) != "act":
                    continue
                src = bank(3 * (n % 2), 3)
                act.wait_ge(job_done, n + 1)
                if job[0] == "z" and job[1] == "x":
                    c = job[2]
                    act.activation(xp(c, A4, SEQ0), src[:, 0:SEQ0], ACT.Copy).then_inc(xp_ready, 1)
                    act.activation(xp(c, B4, SEQ1), src[:, SEQ0:T], ACT.Copy)\
                       .then_inc(act_took, 1)
                elif job[0] == "z" and job[1] == "g":
                    c = job[2]
                    act.activation(gg(c, 0, SEQ0), src[:, 0:SEQ0], ACT.Gelu_apprx_tanh)\
                       .then_inc(gg_ready, 1)
                    act.activation(gg(c, O4, SEQ1), src[:, SEQ0:T], ACT.Gelu_apprx_tanh)\
                       .then_inc(act_took, 1)
                elif job[0] == "z":
                    c = job[2]
                    if c:
                        act.wait_ge(dve_took, c)
                    act.activation(TB[:, 0:T], src[:, 0:T], ACT.Tanh, scale=0.5).then_inc(act_took, 1)
                else:
                    _, kind, d, c = job
                    i = d * CH + c
                    if kind == "a":
                        if c or d:
                            act.wait_ge(gates_used, 2 * c + d)
                        A = AF if d == 0 else AB
                        ins = act.activation(TH[:, 0:L4], src[:, 0:L4], ACT.Tanh, scale=0.5,
                                             bias=half_ba[:, i:i + 1])
                        ins.then_inc(act_took, 1)
                        act.wait_ge(act_took, taken_before(n, "act") + 1)
                        link(act.activation(TH[:, 0:L4], TH[:, 0:L4], ACT.Identity,
                                            scale=sp4[:, i:i + 1], bias=sp4[:, i:i + 1]))
                        link(act.activation(A[:, 0:L4], TH[:, 0:L4], ACT.Exp, scale=-1.0))
                        act.activation(TQ[:, 0:L4], TH[:, 0:L4], ACT.Tanh).then_inc(gates_ready, 1)
                        act.activation(A2[:, 0:L4], A[:, 0:L4], ACT.Square).then_inc(gates_ready, 1)
                    else:
                        act.activation(TX[:, 0:L4], src[:, 0:L4], ACT.Tanh, scale=0.5,
                                       bias=half_bx[:, i:i + 1]).then_inc(act_took, 1)
                        act.wait_ge(q_ready, 2 * c + d + 1)
                        act.activation(A2[:, 0:L4], TQ[:, 0:L4], ACT.Sqrt, scale=0.25)\
                           .then_inc(mult_ready, 1)

            for c in range(CH):
                act.wait_ge(y_ready, c + 1)
                act.wait_ge(gates_used, 2 * CH)
                act.activation(sq_rnn[c][:, 0:L4], gg(c, 0, L4), ACT.Square).then_inc(sq_ready, 1)
                act.wait_ge(sq_ready, c + 1)
                act.activation(gg(c, 0, L4), gg(c, 0, L4), ACT.Copy, scale=col("g_rnn", c))\
                   .then_inc(yg_ready, 1)

            def take(n):
                kind, i, q = B_JOBS[n]
                act.wait_ge(b_done, n + 1)
                if kind in ("k", "v"):
                    act.activation(kvT[:, 2 * i + q, :], bank(6 + n % 2), ACT.Copy).then_inc(b_took, 1)
                    return
                m = STAGED.index(n)
                if m >= 4:
                    act.wait_ge(b_store[m % 4], 16 * (m // 4))
                act.activation(XS[:, (m % 4) * BANK:(m % 4 + 1) * BANK], bank(6 + n % 2), ACT.Copy,
                               scale=1.0 / 16 if kind == "qk" else 1.0).then_inc(b_took, 1)

            def center_squares():
                for c in range(CH):
                    act.wait_ge(cen_ready, c + 1)
                    act.activation(ci(c, 0, L31), xp(c, 0, L31), ACT.Square).then_inc(csq_ready, 1)

            def deviation():
                act.wait_ge(var_done, 1)
                act.activation(TH[:, 0:L31], bank(3, 3)[:, 0:L31], ACT.Sqrt, bias=eps).then_inc(sd_ready, 1)

            def silu_tanh():
                for c in range(CH):
                    act.wait_ge(cn_ready, c + 1)
                    act.activation(ci(c, 0, L31), xp(c, 0, L31), ACT.Tanh, scale=half_lng[:, c:c + 1],
                                   bias=half_lnb[:, c:c + 1]).then_inc(ct_ready, 1)

            def silu_squares():
                for c in range(CH):
                    act.wait_ge(cs_ready, c + 1)
                    act.activation(ci(c, 0, L31), xp(c, 0, L31), ACT.Square).then_inc(c2_ready, 1)
                    act.wait_ge(c2_ready, c + 1)
                    act.activation(xp(c, 0, L31), xp(c, 0, L31), ACT.Copy, scale=hs[:, c:c + 1])\
                       .then_inc(cg_ready, 1)

            for n in range(len(B_JOBS)):
                if n == AT_MEAN + 2:
                    center_squares()
                if n == AT_VAR:
                    deviation()
                if n == AT_VAR + 10:
                    silu_tanh()
                if n == AT_VAR + 16:
                    silu_squares()
                take(n)
            act.wait_ge(stat_done, 2)
            act.activation(rr[:, 0:NB], bank(5)[:, 480:480 + NB], ACT.Sqrt, bias=eps).then_inc(srt_ready, 1)
            act.activation(rr[:, NB:2 * NB], bank(5)[:, 496:496 + NB], ACT.Sqrt, scale=0.25, bias=eps)\
               .then_inc(srt_ready, 1)
            if stop_at_x1:
                return

            def front_norm(b, load, ssq, rsq, normed, src_ready):
                act.wait_ge(load, src_ready)
                act.activation(PF[1], XC, ACT.Square, accum_out=ms)
                act.drain()
                act.activation(rs, ms, ACT.Sqrt, scale=1.0 / D, bias=eps).then_inc(ssq, 1)
                act.wait_ge(rsq, b + 1)
                act.activation(AC, XC, ACT.Copy, scale=rs).then_inc(normed, 1)

            def gelu(r, n):
                act.wait_ge(dot_ready, n + 1)
                act.activation(acts[:, r:r + 1], dots[:, r:r + 1], ACT.Gelu_apprx_tanh).then_inc(act_ready, 1)

            def turns(b, first, count):
                with act.Fori(0, count) as i:
                    for r in range(R):
                        gelu(r, b * PICKS + first * R + i * R + r)

            def walk(b, lo, hi):
                turns(b, lo, hi - lo)
                if hi == GROUPS:
                    for r in TAIL:
                        gelu(r, b * PICKS + GROUPS * R + r - TAIL[0])

            def final(b):
                act.wait_ge(acc_taken, b + 1)
                act.activation(PF[1], XC, ACT.Square, accum_out=fms)
                act.drain()
                act.activation(frs, fms, ACT.Sqrt, scale=1.0 / D, bias=eps).then_inc(ss3, 1)
                act.wait_ge(rs3, b + 1)
                act.activation(AC, XC, ACT.Copy, scale=frs).then_inc(y_norm, 1)

            def front(b, walk):
                walk(1, 3)
                if type(b) is not int:
                    act.wait_ge(y_store, 16 * b - 16)
                front_norm(b, x1_load, ss1, rs1, xa_norm, 16 * b + 16)
                walk(3, 7)
                act.wait_ge(mx_ready, b + 1)
                for h in range(NH):
                    ins = act.activation(BC[:, h * NMEM:(h + 1) * NMEM], PF[1][:, h * NMEM:(h + 1) * NMEM],
                                         ACT.Exp, bias=nmx[:, h:h + 1], accum_out=sme[:, h:h + 1])
                ins.then_inc(p_ready, 1)
                walk(7, 8)
                act.wait_ge(pt_done, b + 1)
                act.activation(AC, PF[0], ACT.Copy).then_inc(pt_ready, 1)
                walk(8, 11)
                front_norm(b, x2_ready, ss2, rs2, xp_norm, b + 1)
                walk(11, 17)
                act.wait_ge(ex_in, b + 1)
                act.activation(CV, CV, ACT.Exp).then_inc(ex_out, 1)
                walk(17, GROUPS)

            front(0, lambda lo, hi: None)
            walk(0, 0, 1)
            front(1, lambda lo, hi: walk(0, lo, hi))
            with act.Fori(1, NB - 1) as b:
                walk(b, 0, 1)
                final(b - 1)
                front(b + 1, lambda lo, hi: walk(b, lo, hi))
            walk(NB - 1, 0, 1)
            final(NB - 2)
            walk(NB - 1, 1, GROUPS)
            final(NB - 1)

        @block.vector
        def _(v):
            own = [0]

            def link(ins):
                own[0] += 1
                ins.then_inc(dve_own, 1)
                v.wait_ge(dve_own, own[0])

            v.memset(eps, EPS).then_inc(eps_ready, 1)

            def recip_rstd(i):
                v.wait_ge(std_ready, i + 1)
                v.reciprocal(rs, rs).then_inc(rstd_ready, 1)

            def evacuate(i):
                v.wait_ge(tr_done, i + 1)
                dst = hT[:, :, i * P:(i + 1) * P] if i < NB else mT[:, :, (i - NB) * P:(i - NB + 1) * P]
                g = col("g_mix" if i < NB else "g_mem", 0, KD)
                v.tensor_tensor(dst, bank(2 * (i % 2), 2).rearrange("p (k t) -> p k t", k=KD),
                                g.unsqueeze(2).to_broadcast([P, KD, P]), ALU.mult).then_inc(ht_ready, 1)

            v.wait_ge(s_cols, 16)
            for i in range(NB + MB):
                recip_rstd(i)
                if i:
                    evacuate(i - 1)
            evacuate(NB + MB - 1)

            v.tensor_scalar(half_ba, col("ba", 0, 8), 0.5, None, ALU.mult)
            v.tensor_scalar(half_bx, col("bx", 0, 8), 0.5, None, ALU.mult)
            v.tensor_scalar(half_lng, col("ln_g", 0, 4), 0.5, None, ALU.mult)
            v.tensor_scalar(half_lnb, col("ln_b", 0, 4), 0.5, None, ALU.mult)
            v.tensor_scalar(hs[:, 0:4], col("g_conv", 0, 4), 0.5, None, ALU.mult)
            link(v.tensor_scalar(col("conv31_w", 0, TAPS31 * CH), col("conv31_w", 0, TAPS31 * CH), 0.5,
                                 None, ALU.mult))
            e, z, z2, acc = sp4, rr[:, 0:8], rr[:, 8:16], hr
            v.wait_ge(sp_exp, 1)
            link(v.tensor_scalar(z, e, 2.0, None, ALU.add))
            link(v.reciprocal(z, z))
            link(v.tensor_tensor(z, z, e, ALU.mult))
            link(v.tensor_tensor(z2, z, z, ALU.mult))
            link(v.tensor_scalar(acc, z2, 8.0 / 19, 8.0 / 17, ALU.mult, ALU.add))
            for n in (15, 13, 11, 9, 7, 5, 3, 1):
                link(v.tensor_tensor(acc, acc, z2, ALU.mult))
                link(v.tensor_scalar(acc, acc, 8.0 / n, None, ALU.add))
            link(v.tensor_tensor(acc, acc, z, ALU.mult))
            link(v.tensor_scalar(z2, col("lam", 0, 8), -4.0, 0.0, ALU.mult, ALU.max))
            v.tensor_tensor(sp4, acc, z2, ALU.add).then_inc(const_half, 1)

            def conv4(c):
                v.wait_ge(xp_ready, c + 1)
                v.wait_ge(act_took, c + 1)
                if c >= 2:
                    v.wait_ge(job_done, JOBS.index(("gate", "x", 1, c - 2)) + 1)
                w = [col("conv4_w", j * CH + c) for j in range(TAPS4)]
                link(v.tensor_scalar(xr(c, 0, L4), xp(c, 0, L4), w[0], col("conv4_b", c), ALU.mult, ALU.add))
                for j in range(1, TAPS4):
                    ins = v.scalar_tensor_tensor(xr(c, 0, L4), xp(c, j, L4), w[j], xr(c, 0, L4),
                                                 ALU.mult, ALU.add)
                    if j < TAPS4 - 1:
                        link(ins)
                ins.then_inc(xr_ready, 1)

            def glu(c):
                n = JOBS.index(("z", "a", c))
                v.wait_ge(job_done, n + 1)
                v.wait_ge(act_took, taken_before(n, "act"))
                v.wait_ge(pads_ready, CH)
                src = bank(3 * (n % 2), 3)
                v.scalar_tensor_tensor(ci(c, A31, SEQ0), TB[:, 0:SEQ0], 1.0, src[:, 0:SEQ0], ALU.add, ALU.mult)
                v.scalar_tensor_tensor(ci(c, B31, SEQ1), TB[:, SEQ0:T], 1.0, src[:, SEQ0:T], ALU.add,
                                       ALU.mult).then_inc(dve_took, 1)

            def lru(c, directions):
                for d in directions:
                    n = 2 * c + d
                    A = AF if d == 0 else AB
                    v.wait_ge(gates_ready, 2 * n + 2)
                    v.scalar_tensor_tensor(TQ[:, 0:L4], A2[:, 0:L4], 1.0, TQ[:, 0:L4], ALU.add, ALU.mult)\
                     .then_inc(q_ready, 1)
                    v.wait_ge(act_took, taken_before(JOBS.index(("gate", "x", d, c)), "act") + 1)
                    link(v.scalar_tensor_tensor(TX[:, 0:L4], TX[:, 0:L4], 1.0, xr(c, 0, L4), ALU.add, ALU.mult))
                    v.wait_ge(mult_ready, n + 1)
                    link(v.tensor_tensor(TX[:, 0:L4], TX[:, 0:L4], A2[:, 0:L4], ALU.mult))
                    if d == 0:
                        v.tensor_tensor_scan(TH[:, 0:SEQ0], A[:, 0:SEQ0], TX[:, 0:SEQ0], 0.0, ALU.mult, ALU.add)
                        link(v.tensor_tensor_scan(TH[:, O4:L4], A[:, O4:L4], TX[:, O4:L4], 0.0, ALU.mult, ALU.add))
                        link(v.tensor_copy(A[:, 0:SEQ0], TH[:, 0:SEQ0]))
                        v.tensor_copy(A[:, O4:L4], TH[:, O4:L4]).then_inc(gates_used, 1)
                    else:
                        def back(t, lo, hi):
                            return t[:, lo:hi][:, ::-1]
                        v.tensor_tensor_scan(back(TH, 0, SEQ0), back(A, 0, SEQ0), back(TX, 0, SEQ0), 0.0,
                                             ALU.mult, ALU.add)
                        link(v.tensor_tensor_scan(back(TH, O4, L4), back(A, O4, L4), back(TX, O4, L4), 0.0,
                                                  ALU.mult, ALU.add))
                        for lo, hi in ((0, SEQ0), (O4, L4)):
                            ins = v.tensor_tensor(AF[:, lo:hi], AF[:, lo:hi], TH[:, lo:hi], ALU.add)
                            link(ins)
                        n_g = JOBS.index(("z", "g", c))
                        v.wait_ge(gg_ready, c + 1)
                        v.wait_ge(act_took, taken_before(n_g, "act") + 1)
                        v.tensor_tensor(gg(c, 0, SEQ0), AF[:, 0:SEQ0], gg(c, 0, SEQ0), ALU.mult)
                        link(v.tensor_tensor(gg(c, O4, SEQ1), AF[:, O4:L4], gg(c, O4, SEQ1), ALU.mult))
                        v.sem_inc(gates_used, 1)
                        v.sem_inc(y_ready, 1)

            conv4(0)
            conv4(1)
            for c in range(CH):
                lru(c, [0])
                glu(c)
                lru(c, [1])
                if c + 2 < CH:
                    conv4(c + 2)
            for c in range(CH):
                w = [col("conv31_w", j * CH + c) for j in range(TAPS31)]
                link(v.tensor_scalar(xp(c, 0, L31), ci(c, 0, L31), w[0], col("conv31_b", c), ALU.mult, ALU.add))
                for j in range(1, TAPS31):
                    ins = v.scalar_tensor_tensor(xp(c, 0, L31), ci(c, j, L31), w[j], xp(c, 0, L31),
                                                 ALU.mult, ALU.add)
                    if j < TAPS31 - 1:
                        link(ins)
                ins.then_inc(conv_ready, 1)
            v.wait_ge(mean_done, 1)
            for c in range(CH):
                v.tensor_tensor(xp(c, 0, L31), xp(c, 0, L31), bank(0, 3)[:, 0:L31], ALU.subtract)\
                 .then_inc(cen_ready, 1)
            v.wait_ge(sd_ready, 1)
            link(v.reciprocal(TH[:, 0:L31], TH[:, 0:L31]))
            for c in range(CH):
                v.wait_ge(csq_ready, c + 1)
                v.tensor_tensor(xp(c, 0, L31), xp(c, 0, L31), TH[:, 0:L31], ALU.mult).then_inc(cn_ready, 1)
            for c in range(CH):
                v.wait_ge(ct_ready, c + 1)
                link(v.tensor_scalar(xp(c, 0, L31), xp(c, 0, L31), col("ln_g", c), col("ln_b", c),
                                     ALU.mult, ALU.add))
                v.scalar_tensor_tensor(xp(c, 0, L31), ci(c, 0, L31), 1.0, xp(c, 0, L31), ALU.add, ALU.mult)\
                 .then_inc(cs_ready, 1)
            v.wait_ge(srt_ready, 2)
            v.reciprocal(rr, rr).then_inc(rr_ready, 1)
            v.wait_ge(rr_ready, 1)

            def mix_out(b):
                x = XS[:, (b % 2) * D:(b % 2 + 1) * D]
                v.wait_ge(x_again[b % 2], 16 * (b // 2 + 1))
                v.wait_ge(out_done, 2 * b + 1)
                v.scalar_tensor_tensor(x, bank(0, 2), rr[:, b:b + 1], x, ALU.mult, ALU.add)\
                 .then_inc(out_took, 1)
                v.wait_ge(out_done, 2 * b + 2)
                v.wait_ge(out_took, 2 * b + 1)
                v.scalar_tensor_tensor(x, bank(2, 2), rr[:, NB + b:NB + b + 1], x, ALU.mult, ALU.add)\
                 .then_inc(x1_made, 1)
                v.wait_ge(x1_made, b + 1)
                v.sem_inc(out_took, 1)

            mix_out(0)
            if stop_at_x1:
                for b in range(1, NB):
                    mix_out(b)
                return

            def hold(s, value):
                v.wait_ge(s, value)
                v.sem_inc(dve_held, 1)

            def pick(b, group, r, k):
                v.wait_ge(row_load[r], (b * USES[r] + group) * 16 + 16)
                v.scalar_tensor_tensor(out=JUNK, in0=ring[r][:, 0:D], scalar=1.0, in1=HC, op0=ALU.mult,
                                       op1=ALU.mult, accum_out=dots[:, r:r + 1]).then_inc(dot_ready, 1)
                v.wait_ge(act_ready, b * PICKS + k + 1)
                v.tensor_scalar(diag[:, r * P:(r + 1) * P], ident[:, :], acts[:, r:r + 1],
                                GATC[:, ds(k, 1)], ALU.mult, ALU.mult).then_inc(diag_ready, 1)

            def turns(b, first, count):
                with v.Fori(0, count) as i:
                    for r in range(R):
                        pick(b, i + first, r, i * R + (first * R + r))

            def walk(b, lo, hi):
                turns(b, lo, hi - lo)
                if hi == GROUPS:
                    for r in TAIL:
                        pick(b, GROUPS, r, GROUPS * R + r - TAIL[0])

            def top16(q):
                src = bank(4 + q)
                sets = [(4 * q + j, src[:, j * NK:(j + 1) * NK], AC[:, j * NK:(j + 1) * NK]) for j in range(4)]
                for m, s, _ in sets:
                    v.max(SV[:, m * 16:m * 16 + 8], s)
                v.drain()
                for m, s, w in sets:
                    v.max_index(SI[:, m * 16:m * 16 + 8], SV[:, m * 16:m * 16 + 8], s)
                    v.match_replace(w, SV[:, m * 16:m * 16 + 8], s, -3e38)
                v.drain()
                for m, _, w in sets:
                    v.max(SV[:, m * 16 + 8:m * 16 + 16], w)
                v.drain()
                for m, _, w in sets:
                    v.max_index(SI[:, m * 16 + 8:m * 16 + 16], SV[:, m * 16 + 8:m * 16 + 16], w)

            def cand_top(h0):
                v.drain()
                hh = [(CAND[:, j * 256:(j + 1) * 256], (h0 + j) * TOPK) for j in range(2)]
                for s, o in hh:
                    v.tensor_tensor(s.rearrange("p (i j) -> p i j", i=TOPK),
                                    SV[:, 2 * o:2 * o + 16].unsqueeze(2).to_broadcast([P, TOPK, TOPK]),
                                    SV[:, 2 * o + 16:2 * o + 32].unsqueeze(1).to_broadcast([P, TOPK, TOPK]),
                                    ALU.add)
                v.drain()
                for s, o in hh:
                    v.max(CV[:, o:o + 8], s)
                v.drain()
                for s, o in hh:
                    v.max_index(CI16[:, o:o + 8], CV[:, o:o + 8], s)
                v.drain()
                for s, o in hh:
                    v.match_replace(s, CV[:, o:o + 8], s, -3e38)
                v.drain()
                for s, o in hh:
                    v.max(CV[:, o + 8:o + 16], s)
                v.drain()
                for s, o in hh:
                    v.max_index(CI16[:, o + 8:o + 16], CV[:, o + 8:o + 16], s)

            def expert_side(side):
                oh = ONEHOT.rearrange("p (k i) -> p k i", i=TOPK)
                oh4 = ONEHOT.rearrange("p (h k i) -> p h k i", h=PH, k=TOPK)
                sif = SIF.rearrange("p (h s i) -> p h s i", h=PH, s=2)
                idx, dst = ((I0, E0), (I1, I1))[side]
                v.tensor_tensor(oh, idx.unsqueeze(2).to_broadcast([P, PICKS, TOPK]),
                                iota[:, :].unsqueeze(1).to_broadcast([P, PICKS, TOPK]), ALU.is_equal)
                v.drain()
                v.tensor_tensor(oh4, oh4, sif[:, :, side, :].unsqueeze(2).to_broadcast([P, PH, TOPK, TOPK]),
                                ALU.mult)
                v.drain()
                v.tensor_reduce(dst, oh, X, ALU.add)
                v.drain()

            def split_position():
                v.tensor_copy(SIF, SI)
                v.tensor_scalar(IDXN, CI16, 4, None, ALU.logical_shift_right)
                v.tensor_scalar(CI16, CI16, 15, None, ALU.bitwise_and)
                v.drain()
                v.tensor_copy(I0, IDXN)
                v.tensor_copy(I1, CI16)
                v.drain()

            def expert_and_gate(b):
                cv = CV.rearrange("p (h k) -> p h k", h=PH)
                v.scalar_tensor_tensor(IDXN, E0, float(NK), I1, ALU.mult, ALU.add)
                v.drain()
                v.wait_ge(ex_out, b + 1)
                v.tensor_reduce(hs, cv, X, ALU.add)
                v.drain()
                v.reciprocal(hr, hs)
                v.drain()
                v.tensor_tensor(GATN.rearrange("p (h k) -> p h k", h=PH), cv,
                                hr.unsqueeze(2).to_broadcast([P, PH, TOPK]), ALU.mult).then_inc(idx_ready, 1)

            def gate_in(b):
                cv = CV.rearrange("p (h k) -> p h k", h=PH)
                v.drain()
                v.tensor_copy(hs, cv[:, :, 0])
                v.drain()
                v.tensor_tensor(cv, cv, hs.unsqueeze(2).to_broadcast([P, PH, TOPK]), ALU.subtract)\
                 .then_inc(ex_in, 1)

            def kt3(t):
                return t.rearrange("p (k t) -> p k t", k=KD)

            def top(b, q):
                hold(s_done, 4 * b + (q + 1))
                if type(b) is int and b == 0 and q == 0:
                    for i in range(2):
                        hold(x1_store[i], 16 * NB // 2)
                top16(q)
                cand_top(2 * q)

            def front(b, walk):
                walk(2, 3)
                v.wait_ge(ss1, b + 1)
                v.reciprocal(rs, rs).then_inc(rs1, 1)
                walk(3, 4)
                v.wait_ge(t1_done, b + 1)
                v.tensor_tensor(kt3(BC), kt3(PF[0]), col("g_xattn", 0, KD).unsqueeze(2).to_broadcast([P, KD, P]),
                                ALU.mult).then_inc(h1_ready, 1)
                walk(4, 7)
                v.wait_ge(sc_done, b + 1)
                v.tensor_reduce(nmx, PF[1].rearrange("p (h m) -> p h m", h=NH), X, ALU.max, negate=True)\
                 .then_inc(mx_ready, 1)
                v.wait_ge(p_ready, b + 1)
                v.reciprocal(rse, sme)
                v.drain()
                v.tensor_tensor(BC.rearrange("p (h m) -> p h m", h=NH), BC.rearrange("p (h m) -> p h m", h=NH),
                                rse.unsqueeze(2).to_broadcast([P, NH, NMEM]), ALU.mult).then_inc(pn_ready, 1)
                walk(7, 11)
                v.wait_ge(xo_done, b + 1)
                v.tensor_tensor(XC, XC, PF[1], ALU.add).then_inc(x2_ready, 1)
                v.wait_ge(ss2, b + 1)
                v.reciprocal(rs, rs).then_inc(rs2, 1)
                walk(11, 12)
                v.wait_ge(gp_load, 16 * b + 16)
                v.wait_ge(xp_norm, b + 1)
                v.tensor_tensor(HN, HN, AC, ALU.mult).then_inc(hn_ready, 1)
                v.wait_ge(t2_done, b + 1)
                v.tensor_tensor(kt3(BC), kt3(PF[0]), col("g_peer", 0, KD).unsqueeze(2).to_broadcast([P, KD, P]),
                                ALU.mult).then_inc(h2_ready, 1)
                hold(x2_store, 16 * b + 16)
                hold(hn_ready, b + 1)
                walk(12, 14)
                top(b, 0)
                walk(14, 15)
                top(b, 1)
                walk(15, 16)
                top(b, 2)
                walk(16, 17)
                top(b, 3)
                gate_in(b)
                walk(17, 18)
                if type(b) is not int or b >= 1:
                    hold(idx_taken, b)
                split_position()
                expert_side(0)
                walk(18, 19)
                expert_side(1)
                expert_and_gate(b)
                walk(19, GROUPS)

            def take_over(b):
                v.wait_ge(idx_ready, b + 1)
                v.tensor_copy(HC, HN).then_inc(h_taken, 1)
                v.tensor_copy(GATC, GATN)
                v.drain()

            def close(b):
                v.wait_ge(row_used, (b + 1) * PICKS + R)
                v.wait_ge(x2_load, 16 * b + 16)
                v.tensor_tensor(XC, XC, ACC, ALU.add).then_inc(acc_taken, 1)

            def final_rstd(b):
                v.wait_ge(ss3, b + 1)
                v.reciprocal(frs, frs).then_inc(rs3, 1)

            def final_gain(b):
                v.wait_ge(gf_load, 16 * b + 16)
                v.wait_ge(y_norm, b + 1)
                v.tensor_tensor(AC, AC, BC, ALU.mult).then_inc(y_ready2, 1)

            def mix_between(lo, hi):
                for b, turn in MIX_TURN.items():
                    if lo <= turn < hi:
                        mix_out(b)

            mix_between(0, 2)
            front(0, mix_between)
            take_over(0)
            walk(0, 0, 2)
            front(1, lambda lo, hi: walk(0, lo, hi))
            close(0)
            take_over(1)
            with v.Fori(1, NB - 1) as b:
                walk(b, 0, 1)
                final_rstd(b - 1)
                walk(b, 1, 2)
                final_gain(b - 1)
                front(b + 1, lambda lo, hi: walk(b, lo, hi))
                close(b)
                take_over(b + 1)
            walk(NB - 1, 0, 1)
            final_rstd(NB - 2)
            final_gain(NB - 2)
            walk(NB - 1, 1, GROUPS)
            close(NB - 1)
            final_rstd(NB - 1)
            final_gain(NB - 1)

        @block.tensor
        def _(t):
            t.wait_ge(ident_ready, 3)
            for i in range(NB + MB):
                t.wait_ge(xn_ready, i + 1)
                if i >= 2:
                    t.wait_ge(ht_ready, i - 1)
                for k in range(KD):
                    ins = t.transpose(ps[:, (i % 2) * 1024 + k * P:(i % 2) * 1024 + (k + 1) * P],
                                      xn_p0[i % 4][:, k * P:(k + 1) * P], ident[:, :])
                ins.then_inc(tr_done, 1)
            t.wait_ge(ht_ready, NB + MB)

            def item(j):
                t.wait_ge(w_load[j % 2], 16 * (j // 2 + 1))
                return RING[:, (j % 2) * 2 * D:(j % 2 + 1) * 2 * D]

            def tiles(total):
                return [(lo, min(BANK, total - lo)) for lo in range(0, total, BANK)]

            t.wait_ge(s_gm, 32)
            zs = 0
            for n, job in enumerate(JOBS):
                if n >= 2:
                    prev = n - 2
                    if taker(JOBS[prev]) == "act":
                        t.wait_ge(act_took, taken_before(prev, "act") + 1)
                    else:
                        t.wait_ge(dve_took, taken_before(prev, "dve") + 1)
                base = 3 * (n % 2) * BANK
                if job[0] == "z":
                    w = item(zs // 2)[:, (zs % 2) * D:(zs % 2 + 1) * D]
                    for lo, size in tiles(T):
                        for k in range(KD):
                            ins = t.matmul(ps[:, base + lo:base + lo + size], w[:, k * P:(k + 1) * P],
                                           hT[:, k, lo:lo + size], start=k == 0, stop=k == KD - 1)
                    ins.then_inc(job_done, 1)
                    zs += 1
                    if zs % 2 == 0:
                        t.wait_ge(job_done, n + 1)
                        t.sem_inc(item_done, 1)
                else:
                    _, kind, d, c = job
                    t.wait_ge(xr_ready, c + 1)
                    m = (0 if kind == "a" else 2 * CH) + d * CH + c
                    for lo, size in tiles(L4):
                        ins = t.matmul(ps[:, base + lo:base + lo + size], gm[:, m, :], xr(c, lo, size),
                                       start=True, stop=True)
                    ins.then_inc(job_done, 1)

            def b_job(n):
                kind, i, q = B_JOBS[n]
                if n >= 2:
                    t.wait_ge(b_took, n - 1)
                o = bank(6 + n % 2)
                if kind in ("k", "v"):
                    for k in range(KD):
                        ins = t.matmul(o, w[:, q * D + k * P:q * D + (k + 1) * P], mT[:, k, :],
                                       start=k == 0, stop=k == KD - 1)
                elif kind == "qk":
                    t.wait_ge(b_took, B_JOBS.index(("qk", 0, 0)))
                    for j in range(2):
                        ins = t.matmul(o, w[:, j * D + q * P:j * D + (q + 1) * P], kvT[:, 2 * i + j, :],
                                       start=j == 0, stop=j == 1)
                elif kind == "vo":
                    t.wait_ge(b_took, B_JOBS.index(("vo", 0, 0)))
                    mem = (q // 2) * P
                    for j in range(2):
                        ins = t.matmul(o, kvT[:, 2 * i + j, mem:mem + P],
                                       w[:, j * D + (q % 2) * BANK:j * D + (q % 2 + 1) * BANK],
                                       start=j == 0, stop=j == 1)
                else:
                    t.wait_ge(s_gm, 48)
                    for dq in range(2):
                        for m in range(2):
                            dd = (2 * q + dq) * P
                            ins = t.matmul(o[:, (2 * dq + m) * P:(2 * dq + m + 1) * P],
                                           w[:, m * D + dd:m * D + dd + P], gm[:, 2 * i + m, :],
                                           start=True, stop=True)
                ins.then_inc(b_done, 1)

            def token_sums(squares, start_of, at_col):
                for b in range(NB):
                    for c in range(CH):
                        ins = t.matmul(bank(5)[:, at_col + b:at_col + b + 1], squares(c, start_of(b), P),
                                       ones512[:, 0:1], start=c == 0, stop=c == CH - 1)
                ins.then_inc(stat_done, 1)

            def channel_means(first, source, signal):
                for lo, size in tiles(L31):
                    for c in range(CH):
                        ins = t.matmul(ps[:, first * BANK + lo:first * BANK + lo + size], ones512[:, :],
                                       source(c, lo, size), start=c == 0, stop=c == CH - 1)
                ins.then_inc(signal, 1)

            def at4(b):
                return b * P if b < NB0 else O4 + (b - NB0) * P

            def at31(b):
                return b * P if b < NB0 else O31 + (b - NB0) * P

            w = None
            t.wait_ge(act_took, taken_before(len(JOBS), "act"))
            for n in range(len(B_JOBS)):
                if n == AT_RNN:
                    t.wait_ge(sq_ready, CH)
                    token_sums(lambda c, lo, size: sq_rnn[c][:, lo:lo + size], at4, 480)
                if n == AT_MEAN:
                    t.wait_ge(conv_ready, CH)
                    channel_means(0, xp, mean_done)
                if n == AT_VAR:
                    t.wait_ge(csq_ready, CH)
                    channel_means(3, ci, var_done)
                if B_JOBS[n][2] == 0:
                    j = Z_ITEMS + sum(job[2] == 0 for job in B_JOBS[:n])
                    if n:
                        t.wait_ge(b_done, n)
                        t.sem_inc(item_done, 1)
                    w = item(j)
                b_job(n)
            t.wait_ge(c2_ready, CH)
            token_sums(ci, at31, 496)

            def mix_out(b):
                for grp in range(2):
                    if b:
                        t.wait_ge(out_took, 2 * b - 1 + grp)
                    for half in range(2):
                        for c in range(CH):
                            lhs = gg(c, at4(b), P) if grp == 0 else xp(c, at31(b), P)
                            ins = t.matmul(bank(2 * grp + half), lhs,
                                           wo_mix[:, grp * CH + c, half * BANK:(half + 1) * BANK],
                                           start=c == 0, stop=c == CH - 1)
                    ins.then_inc(out_done, 1)

            t.wait_ge(wo_load, 16)
            t.wait_ge(yg_ready, CH)
            t.wait_ge(cg_ready, CH)
            t.wait_ge(srt_ready, 2)
            mix_out(0)
            if stop_at_x1:
                for b in range(1, NB):
                    mix_out(b)
                return

            def mix_between(lo, hi):
                for b, turn in MIX_TURN.items():
                    if lo <= turn < hi:
                        mix_out(b)

            def pick(n, r, start, stop):
                t.wait_ge(diag_ready, n + 1)
                for half in range(2):
                    ins = t.matmul(ACC[:, half * BANK:(half + 1) * BANK], diag[:, r * P:(r + 1) * P],
                                   ring[r][:, D + half * BANK:D + (half + 1) * BANK], start=start, stop=stop)
                ins.then_inc(row_used, 1)

            def turn(b, g, start=False):
                for r in range(R):
                    pick(b * PICKS + g * R + r, r, start and r == 0, False)

            def first_turn(b):
                if type(b) is not int or b:
                    t.wait_ge(acc_taken, b)
                turn(b, 0, start=True)

            def turns(b, first, count):
                with t.Fori(0, count) as i:
                    turn(b, i + first)

            def walk(b, lo, hi):
                if lo == 0:
                    first_turn(b)
                    lo = 1
                if hi > lo:
                    turns(b, lo, hi - lo)
                if hi == GROUPS:
                    for r in TAIL:
                        pick(b * PICKS + GROUPS * R + r - TAIL[0], r, False, r == TAIL[-1])

            def transposes(dst, src):
                for k in range(KD):
                    ins = t.transpose(dst[:, k * P:(k + 1) * P], src[:, k * P:(k + 1) * P], ident[:, :])
                return ins

            def product(ends, dst, lhs, w, half):
                for k in range(KD):
                    ins = t.matmul(dst, lhs[:, k * P:(k + 1) * P], w[:, k, half * BANK:(half + 1) * BANK],
                                   start=k == 0, stop=k == KD - 1)
                if ends is not None:
                    ins.then_inc(ends, 1)

            def front(b, walk):
                walk(3, 4)
                t.wait_ge(xa_norm, b + 1)
                transposes(PF[0], AC).then_inc(t1_done, 1)
                walk(4, 5)
                t.wait_ge(h1_ready, b + 1)
                t.wait_ge(qk_load, 16 if type(b) is int else 32)
                product(None, bank(6), BC, qk, 0)
                walk(5, 6)
                product(sc_done, bank(7), BC, qk, 1)
                walk(6, 8)
                t.wait_ge(pn_ready, b + 1)
                transposes(PF[0], BC).then_inc(pt_done, 1)
                walk(8, 9)
                t.wait_ge(pt_ready, b + 1)
                t.wait_ge(vo_load, 16 if type(b) is int else 32)
                product(None, bank(6), AC, vo, 0)
                walk(9, 10)
                product(xo_done, bank(7), AC, vo, 1)
                walk(10, 12)
                t.wait_ge(xp_norm, b + 1)
                transposes(PF[0], AC).then_inc(t2_done, 1)
                walk(12, 13)
                t.wait_ge(h2_ready, b + 1)
                for q in range(4):
                    if type(b) is int and b == 0:
                        t.wait_ge(wpa_load if q < 2 else wpb_load, 16)
                    product(s_done, bank(4 + q), BC, wp[q // 2], q % 2)
                    walk(13 + q, 14 + q)
                walk(17, GROUPS)

            mix_between(0, 3)
            front(0, mix_between)
            t.sem_inc(row_used, R)
            t.wait_ge(x1_made, NB)
            walk(0, 0, 3)
            front(1, lambda lo, hi: walk(0, lo, hi))
            with t.Fori(1, NB - 1) as b:
                walk(b, 0, 3)
                front(b + 1, lambda lo, hi: walk(b, lo, hi))
            walk(NB - 1, 0, GROUPS)


def kernel(**inputs):
    import numpy as np
    import concourse.bacc as bacc
    from concourse.bass_utils import run_bass_kernel_spmd as run
    stop_at_x1 = False

    x = {k: np.asarray(v) for k, v in inputs.items()}
    nc = bacc.Bacc("TRN2", target_bir_lowering=False, num_devices=1)

    def channels(w):
        return w.reshape(-1, P).T

    cols = np.concatenate([channels(x[k][0]) for k in (
        "g_mix", "g_mem", "g_xattn", "g_peer", "conv4_w", "conv4_b", "lru_ba", "lru_bx", "lru_lam",
        "conv31_w", "conv31_b", "conv_ln_g", "conv_ln_b", "g_out_rnn", "g_out_conv")], axis=1)

    def stationary(w):
        return w.reshape(KD, P, -1, P).transpose(2, 1, 0, 3).reshape(-1, P, D)

    w_in = stationary(x["w_in"][0])[[BASE[k] + c for k, c in CHUNKS]]
    w_k = stationary(x["w_xkv"][0][:, :D])
    w_v = stationary(x["w_xkv"][0][:, D:])
    w_q = x["w_xq"][0].T.reshape(KD, P, D)
    w_o = x["w_xo"][0].reshape(KD, P, D)
    w_pq = x["w_pq"][0].T.reshape(2 * PH, P, D)

    def paired(w):
        return w.reshape(-1, 2, P, D).transpose(0, 2, 1, 3).reshape(-1, P, 2 * D)

    items = paired(np.concatenate([w_in, w_k, w_q, w_v, w_o, w_pq]))
    gates = np.stack([x["lru_wa"][0], x["lru_wx"][0]]).reshape(2, 2, CH, 2, 64, 64)\
        .transpose(3, 4, 0, 1, 2, 5).reshape(2, 64, 16, 64)
    arrays = {
        "xm": np.concatenate([x["x_prompt"][0], x["x_sample"][0], x["mem_prompt"][0], x["mem_sample"][0]]),
        "cols": cols, "items": items, "gates": gates,
        "subk": x["peer_sub_keys"][0].reshape(2 * PH, NK, P).transpose(2, 0, 1),
        "w_out": x["w_out"][0],
        "g_peer_row": x["g_peer"][0], "g_final_row": x["g_final"],
        "uv": np.concatenate([x["peer_u"][0], x["peer_v"][0]], axis=1),
    }
    arrays = {f"in_{k}": np.ascontiguousarray(v) for k, v in arrays.items()}
    aps = {k[3:]: nc.dram_tensor(k, v.shape, mybir.dt.from_np(v.dtype), kind="ExternalInput").ap()
           for k, v in arrays.items()}
    aps["out"] = nc.dram_tensor("out_0", (T, D), mybir.dt.float32, kind="ExternalOutput").ap()
    build(nc, aps, stop_at_x1)
    y = run(nc, [arrays], core_ids=[0]).results[0]["out_0"]
    return y[None, :SEQ0], y[None, SEQ0:]
```

```python
import concourse.bass as bass
from concourse import mybir
from contextlib import ExitStack

P = 128
D = 1024
KD = D // P
SEQ0, SEQ1 = 256, 1024
T = SEQ0 + SEQ1
NB = T // P
NB0 = SEQ0 // P
NMEM = 256
MB = 2 * NMEM // P
CH = 4
TAPS4, TAPS31 = 4, 31
NH = 4
PH = 8
NK = 128
TOPK = 16
PICKS = PH * TOPK
EPS = 1e-6
BANK = 512

A4, B4 = 2, 2 + SEQ0 + 2
L4 = SEQ0 + 2 + SEQ1
O4 = SEQ0 + 2
A31, B31 = 15, 15 + SEQ0 + 15
L31 = SEQ0 + 15 + SEQ1
O31 = SEQ0 + 15
PITCH = L31 + 30
TP = L31 + 1

COLS = [("g_mix", KD), ("g_mem", KD), ("g_xattn", KD), ("g_peer", KD), ("conv4_w", TAPS4 * CH),
        ("conv4_b", CH), ("ba", 2 * CH), ("bx", 2 * CH), ("lam", 2 * CH), ("conv31_w", TAPS31 * CH),
        ("conv31_b", CH), ("ln_g", CH), ("ln_b", CH), ("g_rnn", CH), ("g_conv", CH),
        ("g_final", KD)]
COL = {}
NCOL = 0
for _n, _w in COLS:
    COL[_n] = NCOL
    NCOL += _w

CHUNKS = [("x", 0), ("x", 1), ("x", 2), ("x", 3), ("g", 0), ("b", 0), ("a", 0), ("g", 1),
          ("b", 1), ("a", 1), ("g", 2), ("b", 2), ("a", 2), ("g", 3), ("b", 3), ("a", 3)]
BASE = {"x": 0, "g": CH, "a": 2 * CH, "b": 3 * CH}
Z_ITEMS = 8
B_ITEMS = ["k"] * 4 + ["qk"] * 4 + ["v", "w"] * 4 + ["vo", "w"] * 4
B_ITEMS = [(kind, B_ITEMS[:n].count(kind)) for n, kind in enumerate(B_ITEMS)]
ITEMS = Z_ITEMS + len(B_ITEMS)
W_FIRST = Z_ITEMS + B_ITEMS.index(("w", 0))
B_JOBS = [(kind, i, q) for kind, i in B_ITEMS for q in range({"k": 2, "qk": 8, "v": 2, "vo": 8, "w": 4}[kind])]
STAGED = [n for n, job in enumerate(B_JOBS) if job[0] in ("qk", "vo", "w")]
AT_RNN, AT_MEAN, AT_VAR = 14, 73, 82
AT_CENTER, AT_TANH, AT_SILU = (75, 76, 77, 78), (92, 93, 94, 95), (96, 98, 100, 102)
SUM_CONV, SUM_VAR, SUM_SQUARES = (42, 60, 69), (77, 78, 79), (100, 102, 104)

JOBS = []
for _kind, _c in CHUNKS:
    JOBS.append(("z", _kind, _c))
    if _kind in "ba":
        JOBS += [("gate", w, int(_kind == "a"), _c) for w in "ax"]

R = 6
GROUPS = PICKS // R
TAIL = (2, 3)
assert GROUPS * R + len(TAIL) == PICKS
USES = [GROUPS + (r in TAIL) for r in range(R)]


STEADY = dict(norm=3, sc=(4, 5), soft=6, xo=(7.5, 8.5), x2=9.5, tr=10.5, q=(11.5, 12.5, 13.5, 14.5),
              top=(12.5, 14.5, 16.5, 18.5), cand=(13, 15, 17, 19), expert=(13.5, 15.5, 17.5, 19.5))
FIRST = dict(norm=3, sc=(4, 5), soft=6, xo=(7, 8), x2=9, tr=10, q=(11, 0.5, 1.5, 2.5),
             top=(12, 1.5, 3, 4.5), cand=(12.5, 2, 3.5, 5), expert=(13, 2.5, 4, 5.5))
MIX_TURN = {1: 0, 2: 3, 3: 5, 4: 6, 5: 8, 6: 9, 7: 12, 8: 12.5, 9: 13}
MIX_TURN_VECTOR = {**MIX_TURN, 3: 6, 5: 9}
SECOND = dict(norm=6.5, sc=(7.5, 8.5), soft=9.5, xo=(10.5, 11.5), x2=12.5, tr=13.5,
              q=(14, 15, 16, 17), top=(15, 16.5, 18, 19.5), cand=(15.5, 17, 18.5, 20),
              expert=(16, 17.5, 19, 20.5))
Q = 4
QP = PICKS // Q
QUARTER_TURNS = [QP * (q + 1) // R for q in range(Q)]


def taker(job):
    return "dve" if job[:2] == ("z", "a") else "act"


def taken_before(n, engine):
    return sum(taker(j) == engine for j in JOBS[:n])


def build(nc, a):
    f32, u32 = mybir.dt.float32, mybir.dt.uint32
    ALU, ACT = mybir.AluOpType, mybir.ActivationFunctionType
    X = mybir.AxisListType.X
    ds = bass.ds

    qk_d = nc.dram_tensor("qk_scratch", (2, P, KD, NH * NMEM), f32).ap()
    vo_d = nc.dram_tensor("vo_scratch", (2, P, KD, D), f32).ap()
    wp_d = nc.dram_tensor("wp_scratch", (P, KD, 2 * PH * NK), f32).ap()
    x1_d = nc.dram_tensor("x1_scratch", (T, D), f32).ap()

    ctx = ExitStack()
    with ctx:
        def sb(name, cols, dt=f32):
            return ctx.enter_context(nc.sbuf_tensor(name, [P, cols], dt))

        def sem(name):
            return ctx.enter_context(nc.semaphore(name))

        cols = sb("cols", NCOL)
        c_half = sb("c_half", 8 * CH)
        ident, ones512 = sb("ident", P), sb("ones512", P)
        small = sb("small", 64)
        arena = sb("arena", 51444)
        ps = ctx.enter_context(nc.psum_tensor("ps", [P, 8 * BANK], f32))
        at = [0]

        def piece(words, dt=f32):
            s = arena[:, at[0]:at[0] + words]
            at[0] += words
            return s if dt == f32 else s.bitcast(dt)

        HT = piece(KD * T)
        XP = piece(CH * PITCH)
        GG = piece(CH * TP)
        XS = piece(2 * D)
        zone_d = at[0]
        CI = piece(CH * PITCH)
        kv_at = at[0]
        AF, AB = piece(TP), piece(TP)
        XR = piece(2 * TP)
        TH, TQ, A2, TX = (piece(TP) for _ in range(4))
        MT = piece(KD * MB * P)
        RING = piece(2 * 2 * D)
        GM = piece(16 * P)
        TB = piece(TP)
        hT = HT.rearrange("p (k t) -> p k t", k=KD)
        mT = MT.rearrange("p (k t) -> p k t", k=KD)
        wo_mix = HT[:, 0:KD * D].rearrange("p (k n) -> p k n", k=KD)
        gm = GM.rearrange("p (m n) -> p m n", m=16)
        x_slots = [XS[:, 0:D], XS[:, D:2 * D]] + [t[:, 0:D] for t in (TH, TQ, A2, TX, AB, XR, XR[:, TP:])]
        XSLOTS = len(x_slots)
        sq_rnn = [TH, TQ, A2, TX]
        kvT = arena[:, kv_at:kv_at + KD * 2 * NMEM].rearrange("p (k n) -> p k n", k=KD)

        def xp(c, lo, n):
            return XP[:, c * PITCH + lo:c * PITCH + lo + n]

        def ci(c, lo, n):
            return CI[:, c * PITCH + lo:c * PITCH + lo + n]

        def gg(c, lo, n):
            return GG[:, c * TP + lo:c * TP + lo + n]

        def xr(c, lo, n):
            return XR[:, (c % 2) * TP + lo:(c % 2) * TP + lo + n]

        at[0] = 0
        WPB = piece(KD * D)
        GR = piece(R * 2 * D)
        H1 = piece(D)
        IDXC = piece(PICKS, u32)
        GAT1 = piece(PICKS)
        diag = piece(R * P)
        assert at[0] <= zone_d
        at[0] = zone_d
        QK = piece(KD * D)
        VO = piece(KD * D)
        WPA = piece(KD * D)
        H0, XC, AC, BC = (piece(D) for _ in range(4))
        assert at[0] <= 51444
        H = [H0, H1]
        SI = sb("SI", 2 * PH * TOPK, u32)[:, :]
        CI16 = sb("CI16", PICKS, u32)[:, :]
        IDXN = sb("IDXN", PICKS, u32)[:, :]
        GAT = [sb("GAT0", PICKS)[:, :], GAT1]
        iota = sb("iota", TOPK)
        st = sb("st", R, u32)
        dots, acts, gated = sb("dots", R), sb("acts", R), sb("gated", R)
        ring = [GR[:, r * 2 * D:(r + 1) * 2 * D] for r in range(R)]
        qk = QK.rearrange("p (k n) -> p k n", k=KD)
        vo = VO.rearrange("p (k n) -> p k n", k=KD)
        wp = [w.rearrange("p (k n) -> p k n", k=KD) for w in (WPA, WPB)]
        SV, SIF = XC[:, 0:256], XC[:, 256:512]
        CV, I0, I1, E0 = (XC[:, 512 + i * 128:640 + i * 128] for i in range(4))
        HI = E0.bitcast(u32)
        CAND = AC[:, 2 * TOPK * TOPK:]

        def bank(b, n=1):
            return ps[:, b * BANK:(b + n) * BANK]

        def turned(i):
            return bank(4 if i < NB and i % 2 == 0 else 6, 2)

        ACC = [bank(0, 2), bank(2, 2)]
        PF = [bank(4, 2), bank(6, 2)]

        ms, rs = small[:, 0:1], small[:, 1:2]
        eps = small[:, 2:3]
        nmx, sme, rse = small[:, 4:8], small[:, 8:12], small[:, 12:16]
        rr = small[:, 16:36]
        hs, hr = small[:, 36:44], small[:, 44:52]
        fms, frs = small[:, 52:53], small[:, 53:54]

        def col(name, i=0, n=1):
            return cols[:, COL[name] + i:COL[name] + i + n]

        half_ba, half_bx = c_half[:, 0:8], c_half[:, 8:16]
        sp4 = c_half[:, 16:24]
        half_lng, half_lnb = c_half[:, 24:28], c_half[:, 28:32]

        s_cols, s_gm, s_xload = sem("s_cols"), sem("s_gm"), [sem(f"s_xload{i}") for i in range(XSLOTS)]
        ident_ready, gm_zero, pads_ready = sem("ident_ready"), sem("gm_zero"), sem("pads_ready")
        eps_ready = sem("eps_ready")
        std_ready, rstd_ready, xn_ready = sem("std_ready"), sem("rstd_ready"), sem("xn_ready")
        tr_done, ht_ready = sem("tr_done"), sem("ht_ready")
        w_load = [sem(f"w_load{i}") for i in range(2)]
        item_done, wo_load = sem("item_done"), sem("wo_load")
        job_done, act_took, dve_took = sem("job_done"), sem("act_took"), sem("dve_took")
        xp_ready, xr_ready, gg_ready = (sem(n) for n in ("xp_ready", "xr_ready", "gg_ready"))
        const_half, sp_exp = sem("const_half"), sem("sp_exp")
        gates_ready, q_ready, mult_ready = sem("gates_ready"), sem("q_ready"), sem("mult_ready")
        gates_used, y_ready = sem("gates_used"), sem("y_ready")
        b_done, b_took, b_store = sem("b_done"), sem("b_took"), [sem(f"b_store{i}") for i in range(4)]
        sq_ready, stat_done, yg_ready = sem("sq_ready"), sem("stat_done"), sem("yg_ready")
        rnn_summed, conv_summed, var_summed, c2_summed, pool_own = (sem(n) for n in
            ("rnn_summed", "conv_summed", "var_summed", "c2_summed", "pool_own"))
        conv_ready, mean_done, cen_ready = sem("conv_ready"), sem("mean_done"), sem("cen_ready")
        csq_ready, var_done, sd_ready = sem("csq_ready"), sem("var_done"), sem("sd_ready")
        cn_ready, ct_ready, cs_ready, cg_ready = (sem(n) for n in
                                                  ("cn_ready", "ct_ready", "cs_ready", "cg_ready"))
        c2_ready, srt_ready, rr_ready = sem("c2_ready"), sem("srt_ready"), sem("rr_ready")
        x_again = [sem(f"x_again{i}") for i in range(2)]
        out_done = sem("out_done")
        x1_store = [sem(f"x1_store{i}") for i in range(2)]
        act_own, dve_own = sem("act_own"), sem("dve_own")
        qk_load, vo_load, wpa_load, wpb_load = (sem(n) for n in
                                                ("qk_load", "vo_load", "wpa_load", "wpb_load"))
        out_took = sem("out_took")
        x1_load, ss1, rs1, xa_norm, t1_done, h1_ready = (sem(n) for n in
            ("x1_load", "ss1", "rs1", "xa_norm", "t1_done", "h1_ready"))
        sc_done, mx_ready, p_ready, pn_ready = (sem(n) for n in
            ("sc_done", "mx_ready", "p_ready", "pn_ready"))
        pt_done, pt_ready, xo_done, x2_ready = (sem(n) for n in
            ("pt_done", "pt_ready", "xo_done", "x2_ready"))
        x2_kept, ss2, rs2, xp_norm, t2_done, h2_ready = (sem(n) for n in
            ("x2_kept", "ss2", "rs2", "xp_norm", "t2_done", "h2_ready"))
        t3_done, h_ready, s_done, ex_in, ex_out = (sem(n) for n in
            ("t3_done", "h_ready", "s_done", "ex_in", "ex_out"))
        idx_ready, idx_taken, st_ready = (sem(n) for n in ("idx_ready", "idx_taken", "st_ready"))
        row_load = [sem(f"row_load{r}") for r in range(R)]
        dot_ready, diag_ready, row_used = (sem(n) for n in ("dot_ready", "diag_ready", "row_used"))
        pool_held, sp_held, dve_held = sem("pool_held"), sem("sp_held"), sem("dve_held")
        act_held = sem("act_held")
        ss3, rs3, y_norm, gf_diag, gf_rows, y_ready2, y_store = (sem(n) for n in
            ("ss3", "rs3", "y_norm", "gf_diag", "gf_rows", "y_ready2", "y_store"))

        block = ctx.enter_context(nc.Block())

        @block.sync
        def _(sp):
            sp.dma_start(cols[:, :], a["cols"]).then_inc(s_cols, 16)

            def load_x(i):
                if i >= XSLOTS:
                    sp.wait_ge(tr_done, i - XSLOTS + 1)
                sp.dma_start(x_slots[i % XSLOTS], a["xm"][i * P:(i + 1) * P, :]).then_inc(s_xload[i % XSLOTS], 16)

            def load_item(j):
                if j >= 2:
                    sp.wait_ge(item_done, j - 1)
                sp.dma_start(RING[:, (j % 2) * 2 * D:(j % 2 + 1) * 2 * D], a["items"][j])\
                  .then_inc(w_load[j % 2], 16)

            for i in range(4):
                load_x(i)
            load_item(0)
            for i in range(4, XSLOTS):
                load_x(i)
            sp.wait_ge(gm_zero, 1)
            for e in range(2):
                sp.dma_start(gm[64 * e:64 * e + 64, :, 64 * e:64 * e + 64], a["gates"][e])\
                  .then_inc(s_gm, 16)
            load_item(1)
            for i in range(XSLOTS, NB + MB):
                load_x(i)
            for j in range(2, Z_ITEMS + 2):
                load_item(j)
            sp.wait_ge(item_done, Z_ITEMS)
            sp.dma_start(wo_mix, a["w_out"].rearrange("(k p) n -> p k n", p=P)).then_inc(wo_load, 16)
            for j in range(Z_ITEMS + 2, ITEMS):
                if j == W_FIRST:
                    sp.wait_ge(gates_used, 2 * CH)
                    sp.dma_start(gm, a["subk"]).then_inc(s_gm, 16)
                load_item(j)
            sp.wait_ge(rr_ready, 1)
            for i in range(4):
                sp.wait_ge(b_store[i], 16 * len(STAGED) // 4)

            def flat(x):
                return x.rearrange("p k n -> p (k n)")

            for i in range(2):
                sp.wait_ge(x_again[i], 16)
            sp.dma_start(QK, flat(qk_d[0])).then_inc(qk_load, 16)

            def hold(s, value):
                sp.wait_ge(s, value)
                sp.sem_inc(sp_held, 1)

            def load_x1(b):
                if type(b) is not int or b >= 1:
                    hold(idx_ready, Q * b)
                sp.dma_start(XC, x1_d[ds(b * P, P), :]).then_inc(x1_load, 16)

            def store_y(b):
                hold(y_ready2, b + 1)
                sp.dma_start(a["out"][ds(b * P, P), :], AC).then_inc(y_store, 16)

            sp.wait_ge(x1_store[0], 16)
            load_x1(0)
            sp.dma_start(VO, flat(vo_d[0])).then_inc(vo_load, 16)
            sp.dma_start(wp[0], wp_d[:, :, 0:D]).then_inc(wpa_load, 16)
            for i in range(2):
                sp.wait_ge(x1_store[i], 16 * NB // 2)
            sp.dma_start(wp[1], wp_d[:, :, D:2 * D]).then_inc(wpb_load, 16)
            load_x1(1)
            sp.wait_ge(xo_done, 2)
            sp.dma_start(QK, flat(qk_d[1])).then_inc(qk_load, 16)
            sp.dma_start(VO, flat(vo_d[1])).then_inc(vo_load, 16)
            with sp.Fori(1, NB - 1) as b:
                load_x1(b + 1)
                store_y(b - 1)
            store_y(NB - 2)
            store_y(NB - 1)
            sp.wait_ge(y_store, 16 * NB)

        @block.gpsimd
        def _(g):
            g.memset(GM, 0.0).then_inc(gm_zero, 1)
            g.memset(ident[:, :], 0.0).then_inc(pool_held, 1)
            g.memset(ones512[:, :], 1.0 / (CH * P)).then_inc(ident_ready, 1)
            g.iota(iota[:, :], pattern=[[1, TOPK]], base=0, channel_multiplier=0,
                   allow_small_or_imprecise_dtypes=True).then_inc(ident_ready, 1)
            g.wait_ge(pool_held, 1)
            g.affine_select(out=ident[:, :], in_=ident[:, :], compare_op=ALU.not_equal, fill=1.0,
                            base=0, pattern=[[-1, P]], channel_multiplier=1).then_inc(ident_ready, 1)
            for c in range(CH):
                g.memset(xp(c, 0, A4), 0.0)
                g.memset(xp(c, A4 + SEQ0, 2), 0.0)
                g.memset(xp(c, B4 + SEQ1, 1), 0.0)
                g.memset(gg(c, SEQ0, 2), 0.0)
                g.memset(ci(c, 0, A31), 0.0)
                g.memset(ci(c, A31 + SEQ0, 15), 0.0)
                g.memset(ci(c, B31 + SEQ1, 15), 0.0).then_inc(pads_ready, 1)

            own = [0]

            def add(out, x, y, end=None):
                ins = g.tensor_tensor(out, x, y, ALU.add)
                if end is not None:
                    ins.then_inc(end, 1)
                    return
                own[0] += 1
                ins.then_inc(pool_own, 1)
                g.wait_ge(pool_own, own[0])

            first = sq_rnn[0][:, 0:L4]
            for c in range(1, CH):
                g.wait_ge(sq_ready, c + 1)
                add(first, first, sq_rnn[c][:, 0:L4], rnn_summed if c == CH - 1 else None)

            def add_chunk(c, ready, end):
                g.wait_ge(ready, c + 1)
                add(ci(0, 0, L31), ci(0, 0, L31), ci(c, 0, L31), end if c == CH - 1 else None)

            conv_sum = TQ[:, 0:L31]
            for m, n in enumerate(STAGED):
                kind, i, q = B_JOBS[n]
                if n == SUM_CONV[0]:
                    g.wait_ge(conv_ready, 2)
                    add(conv_sum, xp(0, 0, L31), xp(1, 0, L31))
                if n == SUM_CONV[1]:
                    g.wait_ge(conv_ready, 3)
                    add(conv_sum, conv_sum, xp(2, 0, L31))
                if n == SUM_CONV[2]:
                    g.wait_ge(conv_ready, 4)
                    add(conv_sum, conv_sum, xp(3, 0, L31), conv_summed)
                if n in SUM_VAR:
                    add_chunk(SUM_VAR.index(n) + 1, csq_ready, var_summed)
                if n in SUM_SQUARES:
                    add_chunk(SUM_SQUARES.index(n) + 1, c2_ready, c2_summed)
                src = XS[:, (m % 4) * BANK:(m % 4 + 1) * BANK]
                two = src.rearrange("p (m n) -> p m n", m=2)
                g.wait_ge(b_took, n + 1)
                if kind == "qk":
                    dst, src = qk_d.rearrange("g p k n -> p g k n")[:, :, q, i * NMEM:(i + 1) * NMEM], two
                elif kind == "vo":
                    dst = vo_d[q // 4][:, 2 * i + q // 2 % 2, (q % 2) * BANK:(q % 2 + 1) * BANK]
                else:
                    dst, src = wp_d[:, 2 * q:2 * q + 2, i * 256:(i + 1) * 256], two
                g.dma_start(dst, src).then_inc(b_store[m % 4], 16)
            for i in range(4):
                g.wait_ge(b_store[i], 16 * len(STAGED) // 4)

            def x_tile(b):
                return XS[:, (b % 2) * D:(b % 2 + 1) * D]

            for b in range(2):
                g.dma_start(x_tile(b), a["xm"][b * P:(b + 1) * P, :]).then_inc(x_again[b], 16)
            for b in range(NB):
                g.wait_ge(out_took, 4 * b + 4)
                g.dma_start(x1_d[b * P:(b + 1) * P, :], x_tile(b)).then_inc(x1_store[b % 2], 16)
                if b + 2 < NB:
                    g.wait_ge(x1_store[b % 2], 16 * (b // 2 + 1))
                    g.dma_start(x_tile(b), a["xm"][(b + 2) * P:(b + 3) * P, :]).then_inc(x_again[b % 2], 16)
            for i in range(2):
                g.wait_ge(x1_store[i], 16 * NB // 2)

            def hold(s, value):
                g.wait_ge(s, value)
                g.sem_inc(pool_held, 1)

            def gather(b, group, r, tail=False):
                k = group * R + (r - TAIL[0] if tail else r)
                hold(row_used, b * PICKS + k + 1 + (2 if tail or (type(group) is int and r in TAIL) else 0))
                g.tensor_copy(st[:, r:r + 1], IDXC[:, ds(k, 1)]).then_inc(st_ready, 1)
                hold(st_ready, b * PICKS + k + 1)
                g.indirect_dma_start(out=ring[r], out_offset=None, in_=a["uv"],
                                     in_offset=bass.IndirectOffsetOnAxis(ap=st[:, r:r + 1], axis=0))\
                 .then_inc(row_load[r], 16)

            with g.Fori(0, NB) as b:
                for q in range(Q):
                    part = slice(q * QP, (q + 1) * QP)
                    hold(idx_ready, Q * b + (q + 1))
                    g.tensor_copy(IDXC[:, part], IDXN[:, part]).then_inc(idx_taken, 1)
                    hold(idx_taken, Q * b + (q + 1))
                    if q == 0:
                        for r in range(R):
                            gather(b, 0, r)
                    with g.Fori(QUARTER_TURNS[q - 1] if q else 1, QUARTER_TURNS[q]) as group:
                        for r in range(R):
                            gather(b, group, r)
                for r in TAIL:
                    gather(b, GROUPS, r, tail=True)

        @block.scalar
        def _(act):
            own = [0]

            def link(ins):
                own[0] += 1
                ins.then_inc(act_own, 1)
                act.wait_ge(act_own, own[0])

            act.wait_ge(eps_ready, 1)
            for i in range(NB + MB):
                act.wait_ge(s_xload[i % XSLOTS], 16 * (i // XSLOTS + 1))
                if i >= 1:
                    act.wait_ge(rstd_ready, i)
                link(act.activation(AF[:, 0:D], x_slots[i % XSLOTS], ACT.Square, accum_out=ms))
                act.activation(rs, ms, ACT.Sqrt, scale=1.0 / D, bias=eps).then_inc(std_ready, 1)
                act.wait_ge(rstd_ready, i + 1)
                act.activation(x_slots[i % XSLOTS], x_slots[i % XSLOTS], ACT.Copy, scale=rs).then_inc(xn_ready, 1)
            act.wait_ge(s_cols, 16)
            link(act.activation(c_half[:, 16:24], col("lam", 0, 8), ACT.Abs))
            act.activation(c_half[:, 16:24], c_half[:, 16:24], ACT.Exp, scale=-1.0).then_inc(sp_exp, 1)
            act.wait_ge(const_half, 1)
            act.wait_ge(pads_ready, CH)

            for n, job in enumerate(JOBS):
                if taker(job) != "act":
                    continue
                src = bank(3 * (n % 2), 3)
                act.wait_ge(job_done, n + 1)
                if job[0] == "z" and job[1] == "x":
                    c = job[2]
                    act.activation(xp(c, A4, SEQ0), src[:, 0:SEQ0], ACT.Copy).then_inc(xp_ready, 1)
                    act.activation(xp(c, B4, SEQ1), src[:, SEQ0:T], ACT.Copy)\
                       .then_inc(act_took, 1)
                elif job[0] == "z" and job[1] == "g":
                    c = job[2]
                    act.activation(gg(c, 0, SEQ0), src[:, 0:SEQ0], ACT.Gelu_apprx_tanh)\
                       .then_inc(gg_ready, 1)
                    act.activation(gg(c, O4, SEQ1), src[:, SEQ0:T], ACT.Gelu_apprx_tanh)\
                       .then_inc(act_took, 1)
                elif job[0] == "z":
                    c = job[2]
                    if c:
                        act.wait_ge(dve_took, c)
                    act.activation(TB[:, 0:T], src[:, 0:T], ACT.Tanh, scale=0.5).then_inc(act_took, 1)
                else:
                    _, kind, d, c = job
                    i = d * CH + c
                    if kind == "a":
                        if c or d:
                            act.wait_ge(gates_used, 2 * c + d)
                        A = AF if d == 0 else AB
                        ins = act.activation(TH[:, 0:L4], src[:, 0:L4], ACT.Tanh, scale=0.5,
                                             bias=half_ba[:, i:i + 1])
                        ins.then_inc(act_took, 1)
                        act.wait_ge(act_took, taken_before(n, "act") + 1)
                        link(act.activation(TH[:, 0:L4], TH[:, 0:L4], ACT.Identity,
                                            scale=sp4[:, i:i + 1], bias=sp4[:, i:i + 1]))
                        link(act.activation(A[:, 0:L4], TH[:, 0:L4], ACT.Exp, scale=-1.0))
                        act.activation(TQ[:, 0:L4], TH[:, 0:L4], ACT.Tanh).then_inc(gates_ready, 1)
                        act.activation(A2[:, 0:L4], A[:, 0:L4], ACT.Square).then_inc(gates_ready, 1)
                    else:
                        act.activation(TX[:, 0:L4], src[:, 0:L4], ACT.Tanh, scale=0.5,
                                       bias=half_bx[:, i:i + 1]).then_inc(act_took, 1)
                        act.wait_ge(q_ready, 2 * c + d + 1)
                        act.activation(A2[:, 0:L4], TQ[:, 0:L4], ACT.Sqrt, scale=0.25)\
                           .then_inc(mult_ready, 1)

            def rnn_squares(c):
                act.activation(sq_rnn[c][:, 0:L4], gg(c, 0, L4), ACT.Square).then_inc(sq_ready, 1)
                act.wait_ge(sq_ready, c + 1)
                act.activation(gg(c, 0, L4), gg(c, 0, L4), ACT.Copy, scale=col("g_rnn", c))\
                   .then_inc(yg_ready, 1)

            def take(n):
                kind, i, q = B_JOBS[n]
                act.wait_ge(b_done, n + 1)
                if kind in ("k", "v"):
                    act.activation(kvT[:, 2 * i + q, :], bank(6 + n % 2), ACT.Copy).then_inc(b_took, 1)
                    return
                m = STAGED.index(n)
                if m >= 4:
                    act.wait_ge(b_store[m % 4], 16 * (m // 4))
                act.activation(XS[:, (m % 4) * BANK:(m % 4 + 1) * BANK], bank(6 + n % 2), ACT.Copy,
                               scale=1.0 / 16 if kind == "qk" else 1.0).then_inc(b_took, 1)

            def center_squares(c):
                act.wait_ge(cen_ready, c + 1)
                act.activation(ci(c, 0, L31), xp(c, 0, L31), ACT.Square).then_inc(csq_ready, 1)

            def deviation():
                act.wait_ge(var_done, 1)
                act.activation(TH[:, 0:L31], bank(3, 3)[:, 0:L31], ACT.Sqrt, bias=eps).then_inc(sd_ready, 1)

            def silu_tanh(c):
                act.wait_ge(cn_ready, c + 1)
                act.activation(ci(c, 0, L31), xp(c, 0, L31), ACT.Tanh, scale=half_lng[:, c:c + 1],
                               bias=half_lnb[:, c:c + 1]).then_inc(ct_ready, 1)

            def silu_squares(c):
                act.wait_ge(cs_ready, c + 1)
                act.activation(ci(c, 0, L31), xp(c, 0, L31), ACT.Square).then_inc(c2_ready, 1)

            def conv_gain(c):
                act.wait_ge(c2_ready, c + 1)
                act.activation(xp(c, 0, L31), xp(c, 0, L31), ACT.Copy, scale=hs[:, c:c + 1])\
                   .then_inc(cg_ready, 1)

            act.wait_ge(y_ready, CH)
            act.wait_ge(gates_used, 2 * CH)
            for n in range(len(B_JOBS)):
                if 2 <= n < 2 + CH:
                    rnn_squares(n - 2)
                if n in AT_CENTER:
                    center_squares(AT_CENTER.index(n))
                if n == AT_VAR:
                    deviation()
                if n in AT_TANH:
                    silu_tanh(AT_TANH.index(n))
                if n in AT_SILU:
                    silu_squares(AT_SILU.index(n))
                if n - 4 in AT_SILU:
                    conv_gain(AT_SILU.index(n - 4))
                take(n)
            act.wait_ge(stat_done, 2)
            act.activation(rr[:, 0:NB], bank(5)[:, 480:480 + NB], ACT.Sqrt, bias=eps).then_inc(srt_ready, 1)
            act.activation(rr[:, NB:2 * NB], bank(5)[:, 496:496 + NB], ACT.Sqrt, scale=0.25, bias=eps)\
               .then_inc(srt_ready, 1)

            def front_norm(b, load, ssq, rsq, normed, src_ready):
                act.wait_ge(load, src_ready)
                act.activation(PF[1], XC, ACT.Square, accum_out=ms)
                act.drain()
                act.activation(rs, ms, ACT.Sqrt, scale=1.0 / D, bias=eps).then_inc(ssq, 1)
                act.wait_ge(rsq, b + 1)
                act.activation(AC, XC, ACT.Copy, scale=rs).then_inc(normed, 1)

            def hold(s, value):
                act.wait_ge(s, value)
                act.sem_inc(act_held, 1)

            def pick(n, par, k, r):
                act.wait_ge(dot_ready, n + 1)
                act.activation(acts[:, r:r + 1], dots[:, r:r + 1], ACT.Gelu_apprx_tanh)
                act.drain()
                act.activation(gated[:, r:r + 1], GAT[par][:, ds(k, 1)], ACT.Copy, scale=acts[:, r:r + 1])
                act.drain()
                act.activation(diag[:, r * P:(r + 1) * P], ident[:, :], ACT.Copy, scale=gated[:, r:r + 1])\
                   .then_inc(diag_ready, 1)

            def walk(b, par, lo, hi):
                at, end = int(lo * R), int(hi * R)
                while at < end:
                    whole = (end - at) // R if at % R == 0 else 0
                    if whole:
                        with act.Fori(0, whole) as i:
                            for r in range(R):
                                k = i * R + (at + r)
                                pick(b * PICKS + k, par, k, r)
                        at += whole * R
                    else:
                        pick(b * PICKS + at, par, at, at % R)
                        at += 1

            def tail(b, par):
                for r in TAIL:
                    k = GROUPS * R + r - TAIL[0]
                    pick(b * PICKS + k, par, k, r)

            def final(b, par):
                act.wait_ge(row_used, (b + 1) * PICKS + R)
                act.activation(PF[1], ACC[par], ACT.Square, accum_out=fms)
                act.drain()
                act.activation(frs, fms, ACT.Sqrt, scale=1.0 / D, bias=eps).then_inc(ss3, 1)
                act.wait_ge(rs3, b + 1)
                if type(b) is int and b == NB - 1:
                    act.wait_ge(y_store, 16 * b)
                act.activation(AC, ACC[par], ACT.Copy, scale=frs).then_inc(y_norm, 1)

            def attend(b, par, upto, at):
                upto(at["norm"])
                if type(b) is not int:
                    act.wait_ge(y_store, 16 * b - 16)
                front_norm(b, x1_load, ss1, rs1, xa_norm, 16 * b + 16)
                upto(at["soft"])
                act.wait_ge(mx_ready, b + 1)
                for h in range(NH):
                    ins = act.activation(BC[:, h * NMEM:(h + 1) * NMEM], PF[1][:, h * NMEM:(h + 1) * NMEM],
                                         ACT.Exp, bias=nmx[:, h:h + 1], accum_out=sme[:, h:h + 1])
                ins.then_inc(p_ready, 1)
                act.wait_ge(pt_done, b + 1)
                act.activation(AC, PF[0], ACT.Copy).then_inc(pt_ready, 1)
                upto(at["x2"])
                front_norm(b, x2_ready, ss2, rs2, xp_norm, b + 1)
                upto(at["tr"])
                act.wait_ge(t3_done, b + 1)
                act.activation(H[par], PF[1], ACT.Copy).then_inc(h_ready, 1)

            def choose(b, upto, at, lo, hi):
                for q in range(lo, hi):
                    upto(at["expert"][q])
                    act.wait_ge(ex_in, Q * b + (q + 1))
                    part = CV[:, q * QP:(q + 1) * QP]
                    act.activation(part, part, ACT.Exp).then_inc(ex_out, 1)

            def walker(b, par, start=0):
                pos = [start]

                def upto(turn):
                    if turn > pos[0]:
                        walk(b, par, pos[0], turn)
                        pos[0] = turn
                return upto

            attend(0, 0, lambda turn: None, FIRST)
            choose(0, lambda turn: None, FIRST, 0, 1)
            upto = walker(0, 0)
            choose(0, upto, FIRST, 1, Q)
            attend(1, 1, upto, SECOND)
            choose(1, upto, SECOND, 0, Q)
            upto(GROUPS)
            tail(0, 0)
            with act.Fori(0, (NB - 2) // 2) as pair:
                for par in (1, 0):
                    b = pair * 2 + (2 - par)
                    upto = walker(b, par)
                    upto(1)
                    final(b - 1, 1 - par)
                    attend(b + 1, 1 - par, upto, STEADY)
                    choose(b + 1, upto, STEADY, 0, Q)
                    upto(GROUPS)
                    tail(b, par)
            walk(NB - 1, 1, 0, 1)
            final(NB - 2, 0)
            walk(NB - 1, 1, 1, GROUPS)
            tail(NB - 1, 1)
            final(NB - 1, 1)

        @block.vector
        def _(v):
            own = [0]

            def link(ins):
                own[0] += 1
                ins.then_inc(dve_own, 1)
                v.wait_ge(dve_own, own[0])

            v.memset(eps, EPS).then_inc(eps_ready, 1)

            def recip_rstd(i):
                v.wait_ge(std_ready, i + 1)
                v.reciprocal(rs, rs).then_inc(rstd_ready, 1)

            def evacuate(i):
                v.wait_ge(tr_done, i + 1)
                dst = hT[:, :, i * P:(i + 1) * P] if i < NB else mT[:, :, (i - NB) * P:(i - NB + 1) * P]
                g = col("g_mix" if i < NB else "g_mem", 0, KD)
                v.tensor_tensor(dst, turned(i).rearrange("p (k t) -> p k t", k=KD),
                                g.unsqueeze(2).to_broadcast([P, KD, P]), ALU.mult).then_inc(ht_ready, 1)

            v.wait_ge(s_cols, 16)
            behind = {i: i + (1 if i < 5 else 2 if i < 9 else 3) for i in range(NB)}
            for i in range(NB + MB):
                recip_rstd(i)
                for j in range(NB):
                    if behind[j] == i:
                        evacuate(j)

            v.tensor_scalar(half_ba, col("ba", 0, 8), 0.5, None, ALU.mult)
            v.tensor_scalar(half_bx, col("bx", 0, 8), 0.5, None, ALU.mult)
            v.tensor_scalar(half_lng, col("ln_g", 0, 4), 0.5, None, ALU.mult)
            v.tensor_scalar(half_lnb, col("ln_b", 0, 4), 0.5, None, ALU.mult)
            v.tensor_scalar(col("g_final", 0, KD), col("g_final", 0, KD), float(CH * P), None, ALU.mult)
            v.tensor_scalar(hs[:, 0:4], col("g_conv", 0, 4), 0.5, None, ALU.mult)
            link(v.tensor_scalar(col("conv31_w", 0, TAPS31 * CH), col("conv31_w", 0, TAPS31 * CH), 0.5,
                                 None, ALU.mult))
            e, z, z2, acc = sp4, rr[:, 0:8], rr[:, 8:16], hr
            v.wait_ge(sp_exp, 1)
            link(v.tensor_scalar(z, e, 2.0, None, ALU.add))
            link(v.reciprocal(z, z))
            link(v.tensor_tensor(z, z, e, ALU.mult))
            link(v.tensor_tensor(z2, z, z, ALU.mult))
            link(v.tensor_scalar(acc, z2, 8.0 / 19, 8.0 / 17, ALU.mult, ALU.add))
            for n in (15, 13, 11, 9, 7, 5, 3, 1):
                link(v.tensor_tensor(acc, acc, z2, ALU.mult))
                link(v.tensor_scalar(acc, acc, 8.0 / n, None, ALU.add))
            link(v.tensor_tensor(acc, acc, z, ALU.mult))
            link(v.tensor_scalar(z2, col("lam", 0, 8), -4.0, 0.0, ALU.mult, ALU.max))
            v.tensor_tensor(sp4, acc, z2, ALU.add).then_inc(const_half, 1)
            for i in range(NB, NB + MB):
                evacuate(i)

            def conv4(c):
                v.wait_ge(xp_ready, c + 1)
                v.wait_ge(act_took, c + 1)
                if c >= 2:
                    v.wait_ge(job_done, JOBS.index(("gate", "x", 1, c - 2)) + 1)
                w = [col("conv4_w", j * CH + c) for j in range(TAPS4)]
                link(v.tensor_scalar(xr(c, 0, L4), xp(c, 0, L4), w[0], col("conv4_b", c), ALU.mult, ALU.add))
                for j in range(1, TAPS4):
                    ins = v.scalar_tensor_tensor(xr(c, 0, L4), xp(c, j, L4), w[j], xr(c, 0, L4),
                                                 ALU.mult, ALU.add)
                    if j < TAPS4 - 1:
                        link(ins)
                ins.then_inc(xr_ready, 1)

            def glu(c):
                n = JOBS.index(("z", "a", c))
                v.wait_ge(job_done, n + 1)
                v.wait_ge(act_took, taken_before(n, "act"))
                v.wait_ge(pads_ready, CH)
                src = bank(3 * (n % 2), 3)
                v.scalar_tensor_tensor(ci(c, A31, SEQ0), TB[:, 0:SEQ0], 1.0, src[:, 0:SEQ0], ALU.add, ALU.mult)
                v.scalar_tensor_tensor(ci(c, B31, SEQ1), TB[:, SEQ0:T], 1.0, src[:, SEQ0:T], ALU.add,
                                       ALU.mult).then_inc(dve_took, 1)

            def lru(c, directions):
                for d in directions:
                    n = 2 * c + d
                    A = AF if d == 0 else AB
                    v.wait_ge(gates_ready, 2 * n + 2)
                    v.scalar_tensor_tensor(TQ[:, 0:L4], A2[:, 0:L4], 1.0, TQ[:, 0:L4], ALU.add, ALU.mult)\
                     .then_inc(q_ready, 1)
                    v.wait_ge(act_took, taken_before(JOBS.index(("gate", "x", d, c)), "act") + 1)
                    link(v.scalar_tensor_tensor(TX[:, 0:L4], TX[:, 0:L4], 1.0, xr(c, 0, L4), ALU.add, ALU.mult))
                    v.wait_ge(mult_ready, n + 1)
                    link(v.tensor_tensor(TX[:, 0:L4], TX[:, 0:L4], A2[:, 0:L4], ALU.mult))
                    if d == 0:
                        v.tensor_tensor_scan(TH[:, 0:SEQ0], A[:, 0:SEQ0], TX[:, 0:SEQ0], 0.0, ALU.mult, ALU.add)
                        link(v.tensor_tensor_scan(TH[:, O4:L4], A[:, O4:L4], TX[:, O4:L4], 0.0, ALU.mult, ALU.add))
                        link(v.tensor_copy(A[:, 0:SEQ0], TH[:, 0:SEQ0]))
                        v.tensor_copy(A[:, O4:L4], TH[:, O4:L4]).then_inc(gates_used, 1)
                    else:
                        def back(t, lo, hi):
                            return t[:, lo:hi][:, ::-1]
                        v.tensor_tensor_scan(back(TH, 0, SEQ0), back(A, 0, SEQ0), back(TX, 0, SEQ0), 0.0,
                                             ALU.mult, ALU.add)
                        link(v.tensor_tensor_scan(back(TH, O4, L4), back(A, O4, L4), back(TX, O4, L4), 0.0,
                                                  ALU.mult, ALU.add))
                        for lo, hi in ((0, SEQ0), (O4, L4)):
                            ins = v.tensor_tensor(AF[:, lo:hi], AF[:, lo:hi], TH[:, lo:hi], ALU.add)
                            link(ins)
                        n_g = JOBS.index(("z", "g", c))
                        v.wait_ge(gg_ready, c + 1)
                        v.wait_ge(act_took, taken_before(n_g, "act") + 1)
                        v.tensor_tensor(gg(c, 0, SEQ0), AF[:, 0:SEQ0], gg(c, 0, SEQ0), ALU.mult)
                        link(v.tensor_tensor(gg(c, O4, SEQ1), AF[:, O4:L4], gg(c, O4, SEQ1), ALU.mult))
                        v.sem_inc(gates_used, 1)
                        v.sem_inc(y_ready, 1)

            conv4(0)
            conv4(1)
            for c in range(CH):
                lru(c, [0])
                glu(c)
                lru(c, [1])
                if c + 2 < CH:
                    conv4(c + 2)
            for c in range(CH):
                w = [col("conv31_w", j * CH + c) for j in range(TAPS31)]
                link(v.tensor_scalar(xp(c, 0, L31), ci(c, 0, L31), w[0], col("conv31_b", c), ALU.mult, ALU.add))
                for j in range(1, TAPS31):
                    ins = v.scalar_tensor_tensor(xp(c, 0, L31), ci(c, j, L31), w[j], xp(c, 0, L31),
                                                 ALU.mult, ALU.add)
                    if j < TAPS31 - 1:
                        link(ins)
                ins.then_inc(conv_ready, 1)
            v.wait_ge(mean_done, 1)
            for c in range(CH):
                v.tensor_tensor(xp(c, 0, L31), xp(c, 0, L31), bank(0, 3)[:, 0:L31], ALU.subtract)\
                 .then_inc(cen_ready, 1)
            v.wait_ge(sd_ready, 1)
            link(v.reciprocal(TH[:, 0:L31], TH[:, 0:L31]))
            for c in range(CH):
                v.wait_ge(csq_ready, c + 1)
                v.tensor_tensor(xp(c, 0, L31), xp(c, 0, L31), TH[:, 0:L31], ALU.mult).then_inc(cn_ready, 1)
            for c in range(CH):
                v.wait_ge(ct_ready, c + 1)
                link(v.tensor_scalar(xp(c, 0, L31), xp(c, 0, L31), col("ln_g", c), col("ln_b", c),
                                     ALU.mult, ALU.add))
                v.scalar_tensor_tensor(xp(c, 0, L31), ci(c, 0, L31), 1.0, xp(c, 0, L31), ALU.add, ALU.mult)\
                 .then_inc(cs_ready, 1)
            v.wait_ge(srt_ready, 2)
            v.reciprocal(rr, rr).then_inc(rr_ready, 1)
            v.wait_ge(rr_ready, 1)

            def mix_out(b):
                v.wait_ge(x_again[b % 2], 16 * (b // 2 + 1))
                for grp in range(2):
                    for half in range(2):
                        n = 4 * b + 2 * grp + half
                        x = XS[:, (b % 2) * D + half * BANK:(b % 2) * D + (half + 1) * BANK]
                        v.wait_ge(out_done, n + 1)
                        if grp:
                            v.wait_ge(out_took, n - 1)
                        v.scalar_tensor_tensor(x, bank(2 + half), rr[:, grp * NB + b:grp * NB + b + 1], x,
                                               ALU.mult, ALU.add).then_inc(out_took, 1)

            mix_out(0)

            def hold(s, value):
                v.wait_ge(s, value)
                v.sem_inc(dve_held, 1)

            def pick(b, par, group, r):
                v.wait_ge(row_load[r], (b * USES[r] + group) * 16 + 16)
                v.scalar_tensor_tensor(out=ring[r][:, 0:D], in0=ring[r][:, 0:D], scalar=1.0, in1=H[par],
                                       op0=ALU.mult, op1=ALU.mult, accum_out=dots[:, r:r + 1])\
                 .then_inc(dot_ready, 1)

            def walk(b, par, lo, hi):
                at, end = int(lo * R), int(hi * R)
                while at < end:
                    whole = (end - at) // R if at % R == 0 else 0
                    if whole:
                        with v.Fori(0, whole) as i:
                            for r in range(R):
                                pick(b, par, i + at // R, r)
                        at += whole * R
                    else:
                        pick(b, par, at // R, at % R)
                        at += 1

            def tail(b, par):
                for r in TAIL:
                    pick(b, par, GROUPS, r)

            def top16(q):
                src = bank(4 + q)
                sets = [(4 * q + j, src[:, j * NK:(j + 1) * NK], AC[:, j * NK:(j + 1) * NK]) for j in range(4)]
                for m, s, _ in sets:
                    v.max(SV[:, m * 16:m * 16 + 8], s)
                v.drain()
                for m, s, w in sets:
                    v.max_index(SI[:, m * 16:m * 16 + 8], SV[:, m * 16:m * 16 + 8], s)
                    v.match_replace(w, SV[:, m * 16:m * 16 + 8], s, -3e38)
                v.drain()
                for m, _, w in sets:
                    v.max(SV[:, m * 16 + 8:m * 16 + 16], w)
                v.drain()
                for m, _, w in sets:
                    v.max_index(SI[:, m * 16 + 8:m * 16 + 16], SV[:, m * 16 + 8:m * 16 + 16], w)

            def cand_top(h0):
                v.drain()
                hh = [(CAND[:, j * 256:(j + 1) * 256], (h0 + j) * TOPK) for j in range(2)]
                for s, o in hh:
                    v.tensor_tensor(s.rearrange("p (i j) -> p i j", i=TOPK),
                                    SV[:, 2 * o:2 * o + 16].unsqueeze(2).to_broadcast([P, TOPK, TOPK]),
                                    SV[:, 2 * o + 16:2 * o + 32].unsqueeze(1).to_broadcast([P, TOPK, TOPK]),
                                    ALU.add)
                v.drain()
                for s, o in hh:
                    v.max(CV[:, o:o + 8], s)
                v.drain()
                for s, o in hh:
                    v.max_index(CI16[:, o:o + 8], CV[:, o:o + 8], s)
                v.drain()
                for s, o in hh:
                    v.match_replace(s, CV[:, o:o + 8], s, -3e38)
                v.drain()
                for s, o in hh:
                    v.max(CV[:, o + 8:o + 16], s)
                v.drain()
                for s, o in hh:
                    v.max_index(CI16[:, o + 8:o + 16], CV[:, o + 8:o + 16], s)

            def expert_side(side, q):
                oh = CAND.rearrange("p (k i) -> p k i", i=TOPK)
                oh4 = CAND.rearrange("p (h k i) -> p h k i", h=2, k=TOPK)
                sif = SIF.rearrange("p (h s i) -> p h s i", h=PH, s=2)[:, 2 * q:2 * q + 2, side, :]
                idx, dst = [t[:, q * QP:(q + 1) * QP] for t in ((I0, E0), (I1, I1))[side]]
                v.tensor_tensor(oh, idx.unsqueeze(2).to_broadcast([P, QP, TOPK]),
                                iota[:, :].unsqueeze(1).to_broadcast([P, QP, TOPK]), ALU.is_equal)
                v.drain()
                v.tensor_tensor(oh4, oh4, sif.unsqueeze(2).to_broadcast([P, 2, TOPK, TOPK]), ALU.mult)
                v.drain()
                v.tensor_reduce(dst, oh, X, ALU.add)
                v.drain()

            def experts(q):
                part = slice(q * QP, (q + 1) * QP)
                both = slice(2 * q * QP, 2 * (q + 1) * QP)
                v.tensor_copy(SIF[:, both], SI[:, both])
                v.tensor_scalar(HI[:, part], CI16[:, part], 4, None, ALU.logical_shift_right)
                v.tensor_scalar(CI16[:, part], CI16[:, part], 15, None, ALU.bitwise_and)
                v.drain()
                v.tensor_copy(I0[:, part], HI[:, part])
                v.tensor_copy(I1[:, part], CI16[:, part])
                v.drain()
                expert_side(0, q)
                expert_side(1, q)
                v.scalar_tensor_tensor(IDXN[:, part], E0[:, part], float(NK), I1[:, part], ALU.mult, ALU.add)

            def gate_in(q):
                cv = CV.rearrange("p (h k) -> p h k", h=PH)[:, 2 * q:2 * q + 2]
                v.drain()
                v.tensor_copy(hs[:, 2 * q:2 * q + 2], cv[:, :, 0])
                v.drain()
                v.tensor_tensor(cv, cv, hs[:, 2 * q:2 * q + 2].unsqueeze(2).to_broadcast([P, 2, TOPK]),
                                ALU.subtract).then_inc(ex_in, 1)

            def gates(b, par, q):
                heads = slice(2 * q, 2 * q + 2)
                cv = CV.rearrange("p (h k) -> p h k", h=PH)[:, heads]
                v.wait_ge(ex_out, Q * b + (q + 1))
                v.tensor_reduce(hs[:, heads], cv, X, ALU.add)
                v.drain()
                v.reciprocal(hr[:, heads], hs[:, heads])
                v.drain()
                v.tensor_tensor(GAT[par].rearrange("p (h k) -> p h k", h=PH)[:, heads], cv,
                                hr[:, heads].unsqueeze(2).to_broadcast([P, 2, TOPK]), ALU.mult)\
                 .then_inc(idx_ready, 1)

            def kt3(t):
                return t.rearrange("p (k t) -> p k t", k=KD)

            def attend(b, upto, at):
                upto(at["norm"])
                v.wait_ge(ss1, b + 1)
                v.reciprocal(rs, rs).then_inc(rs1, 1)
                v.wait_ge(t1_done, b + 1)
                v.tensor_tensor(kt3(BC), kt3(PF[0]), col("g_xattn", 0, KD).unsqueeze(2).to_broadcast([P, KD, P]),
                                ALU.mult).then_inc(h1_ready, 1)
                upto(at["soft"])
                v.wait_ge(sc_done, b + 1)
                v.tensor_reduce(nmx, PF[1].rearrange("p (h m) -> p h m", h=NH), X, ALU.max, negate=True)\
                 .then_inc(mx_ready, 1)
                v.wait_ge(p_ready, b + 1)
                v.reciprocal(rse, sme)
                v.drain()
                v.tensor_tensor(BC.rearrange("p (h m) -> p h m", h=NH), BC.rearrange("p (h m) -> p h m", h=NH),
                                rse.unsqueeze(2).to_broadcast([P, NH, NMEM]), ALU.mult).then_inc(pn_ready, 1)
                upto(at["x2"])
                v.wait_ge(xo_done, b + 1)
                v.tensor_tensor(XC, XC, PF[1], ALU.add).then_inc(x2_ready, 1)
                v.wait_ge(ss2, b + 1)
                v.reciprocal(rs, rs).then_inc(rs2, 1)
                upto(at["tr"])
                v.wait_ge(t2_done, b + 1)
                v.tensor_tensor(kt3(BC), kt3(PF[0]), col("g_peer", 0, KD).unsqueeze(2).to_broadcast([P, KD, P]),
                                ALU.mult).then_inc(h2_ready, 1)

            def choose(b, par, upto, at, steps):
                for step, q in steps:
                    upto(at[step][q])
                    if step == "top":
                        hold(s_done, Q * b + (q + 1))
                        if q == 0:
                            hold(x2_kept, b + 1)
                        top16(q)
                    elif step == "cand":
                        cand_top(2 * q)
                        gate_in(q)
                    else:
                        if type(b) is not int or b >= 1:
                            hold(idx_taken, Q * b + (q + 1 - Q))
                        experts(q)
                        gates(b, par, q)

            def take_over(b):
                hold(h_ready, b + 1)

            def final_rstd(b):
                v.wait_ge(ss3, b + 1)
                v.reciprocal(frs, frs).then_inc(rs3, 1)

            def final_diag():
                v.tensor_tensor(kt3(BC), ident[:, :].unsqueeze(1).to_broadcast([P, KD, P]),
                                col("g_final", 0, KD).unsqueeze(2).to_broadcast([P, KD, P]), ALU.mult)\
                 .then_inc(gf_diag, 1)

            def final_gain(b):
                v.wait_ge(y_norm, b + 1)
                v.wait_ge(gf_rows, b + 1)
                v.tensor_tensor(AC, AC, PF[0], ALU.mult).then_inc(y_ready2, 1)

            def mixer():
                left = sorted(MIX_TURN_VECTOR)

                def upto(turn):
                    while left and MIX_TURN_VECTOR[left[0]] < turn:
                        mix_out(left.pop(0))
                return upto

            def walker(b, par):
                pos = [0]

                def upto(turn):
                    if turn > pos[0]:
                        walk(b, par, pos[0], turn)
                        pos[0] = turn
                return upto

            steps = [(step, q) for q in range(Q) for step in ("top", "cand", "expert")]
            upto = mixer()
            attend(0, upto, FIRST)
            choose(0, 0, upto, FIRST, steps[:3])
            upto(GROUPS)
            take_over(0)
            upto = walker(0, 0)
            choose(0, 0, upto, FIRST, steps[3:])
            attend(1, upto, SECOND)
            choose(1, 1, upto, SECOND, steps)
            upto(GROUPS)
            tail(0, 0)
            take_over(1)
            with v.Fori(0, (NB - 2) // 2) as pair:
                for par in (1, 0):
                    b = pair * 2 + (2 - par)
                    upto = walker(b, par)
                    final_diag()
                    upto(1)
                    final_rstd(b - 1)
                    upto(2)
                    final_gain(b - 1)
                    attend(b + 1, upto, STEADY)
                    choose(b + 1, 1 - par, upto, STEADY, steps)
                    upto(GROUPS)
                    tail(b, par)
                    take_over(b + 1)
            final_diag()
            walk(NB - 1, 1, 0, 1)
            final_rstd(NB - 2)
            walk(NB - 1, 1, 1, 2)
            final_gain(NB - 2)
            final_diag()
            walk(NB - 1, 1, 2, GROUPS)
            tail(NB - 1, 1)
            final_rstd(NB - 1)
            final_gain(NB - 1)

        @block.tensor
        def _(t):
            t.wait_ge(ident_ready, 3)

            def turn_block(i):
                t.wait_ge(xn_ready, i + 1)
                if i >= 2:
                    t.wait_ge(ht_ready, i - 1 if i < NB else i)
                for k in range(KD):
                    ins = t.transpose(turned(i)[:, k * P:(k + 1) * P], x_slots[i % XSLOTS][:, k * P:(k + 1) * P],
                                      ident[:, :])
                ins.then_inc(tr_done, 1)


            def item(j):
                t.wait_ge(w_load[j % 2], 16 * (j // 2 + 1))
                return RING[:, (j % 2) * 2 * D:(j % 2 + 1) * 2 * D]

            def tiles(total):
                return [(lo, min(BANK, total - lo)) for lo in range(0, total, BANK)]

            zs, blocks = 0, 0
            for n, job in enumerate(JOBS):
                if 0 < n <= MB:
                    turn_block(NB + n - 1)
                if n >= 2:
                    prev = n - 2
                    if taker(JOBS[prev]) == "act":
                        t.wait_ge(act_took, taken_before(prev, "act") + 1)
                    else:
                        t.wait_ge(dve_took, taken_before(prev, "dve") + 1)
                base = 3 * (n % 2) * BANK
                if job[0] == "z":
                    w = item(zs // 2)[:, (zs % 2) * D:(zs % 2 + 1) * D]
                    for lo, size in tiles(T):
                        if n == 0:
                            need = (lo + size) // P
                            while blocks < min(need + 1, NB):
                                turn_block(blocks)
                                blocks += 1
                            t.wait_ge(ht_ready, need)
                        for k in range(KD):
                            ins = t.matmul(ps[:, base + lo:base + lo + size], w[:, k * P:(k + 1) * P],
                                           hT[:, k, lo:lo + size], start=k == 0, stop=k == KD - 1)
                    ins.then_inc(job_done, 1)
                    zs += 1
                    if zs % 2 == 0:
                        t.wait_ge(job_done, n + 1)
                        t.sem_inc(item_done, 1)
                else:
                    _, kind, d, c = job
                    t.wait_ge(s_gm, 32)
                    t.wait_ge(xr_ready, c + 1)
                    m = (0 if kind == "a" else 2 * CH) + d * CH + c
                    for lo, size in tiles(L4):
                        ins = t.matmul(ps[:, base + lo:base + lo + size], gm[:, m, :], xr(c, lo, size),
                                       start=True, stop=True)
                    ins.then_inc(job_done, 1)

            def b_job(n):
                kind, i, q = B_JOBS[n]
                if n >= 2:
                    t.wait_ge(b_took, n - 1)
                o = bank(6 + n % 2)
                if kind in ("k", "v"):
                    for k in range(KD):
                        ins = t.matmul(o, w[:, q * D + k * P:q * D + (k + 1) * P], mT[:, k, :],
                                       start=k == 0, stop=k == KD - 1)
                elif kind == "qk":
                    t.wait_ge(b_took, B_JOBS.index(("qk", 0, 0)))
                    for j in range(2):
                        ins = t.matmul(o, w[:, j * D + q * P:j * D + (q + 1) * P], kvT[:, 2 * i + j, :],
                                       start=j == 0, stop=j == 1)
                elif kind == "vo":
                    t.wait_ge(b_took, B_JOBS.index(("vo", 0, 0)))
                    mem = (q // 2) * P
                    for j in range(2):
                        ins = t.matmul(o, kvT[:, 2 * i + j, mem:mem + P],
                                       w[:, j * D + (q % 2) * BANK:j * D + (q % 2 + 1) * BANK],
                                       start=j == 0, stop=j == 1)
                else:
                    t.wait_ge(s_gm, 48)
                    for dq in range(2):
                        for m in range(2):
                            dd = (2 * q + dq) * P
                            ins = t.matmul(o[:, (2 * dq + m) * P:(2 * dq + m + 1) * P],
                                           w[:, m * D + dd:m * D + dd + P], gm[:, 2 * i + m, :],
                                           start=True, stop=True)
                ins.then_inc(b_done, 1)

            def token_sums(squares, start_of, at_col):
                for b in range(NB):
                    ins = t.matmul(bank(5)[:, at_col + b:at_col + b + 1],
                                   squares[:, start_of(b):start_of(b) + P], ones512[:, 0:1],
                                   start=True, stop=True)
                ins.then_inc(stat_done, 1)

            def channel_means(first, source, signal):
                for lo, size in tiles(L31):
                    ins = t.matmul(ps[:, first * BANK + lo:first * BANK + lo + size], ones512[:, :],
                                   source[:, lo:lo + size], start=True, stop=True)
                ins.then_inc(signal, 1)

            def at4(b):
                return b * P if b < NB0 else O4 + (b - NB0) * P

            def at31(b):
                return b * P if b < NB0 else O31 + (b - NB0) * P

            w = None
            t.wait_ge(ht_ready, NB + MB)
            for n in range(len(B_JOBS)):
                if n == AT_RNN:
                    t.wait_ge(act_took, taken_before(len(JOBS), "act"))
                    t.wait_ge(rnn_summed, 1)
                    token_sums(sq_rnn[0], at4, 480)
                if n == AT_MEAN:
                    t.wait_ge(conv_summed, 1)
                    channel_means(0, TQ, mean_done)
                if n == AT_VAR:
                    t.wait_ge(var_summed, 1)
                    channel_means(3, ci(0, 0, L31), var_done)
                if B_JOBS[n][2] == 0:
                    j = Z_ITEMS + sum(job[2] == 0 for job in B_JOBS[:n])
                    if n:
                        t.wait_ge(b_done, n)
                        t.sem_inc(item_done, 1)
                    w = item(j)
                b_job(n)
            t.wait_ge(c2_summed, 1)
            token_sums(ci(0, 0, L31), at31, 496)

            def mix_out(b):
                for grp in range(2):
                    for half in range(2):
                        n = 4 * b + 2 * grp + half
                        if n >= 2:
                            t.wait_ge(out_took, n - 1)
                        for c in range(CH):
                            lhs = gg(c, at4(b), P) if grp == 0 else xp(c, at31(b), P)
                            ins = t.matmul(bank(2 + half), lhs,
                                           wo_mix[:, grp * CH + c, half * BANK:(half + 1) * BANK],
                                           start=c == 0, stop=c == CH - 1)
                        ins.then_inc(out_done, 1)

            t.wait_ge(wo_load, 16)
            t.wait_ge(yg_ready, CH)
            t.wait_ge(cg_ready, CH)
            t.wait_ge(srt_ready, 2)
            mix_out(0)

            def pick(n, par, r, stop=False):
                t.wait_ge(diag_ready, n + 1)
                for half in range(2):
                    ins = t.matmul(ACC[par][:, half * BANK:(half + 1) * BANK], diag[:, r * P:(r + 1) * P],
                                   ring[r][:, D + half * BANK:D + (half + 1) * BANK], start=False, stop=stop)
                ins.then_inc(row_used, 1)

            def walk(b, par, lo, hi):
                at, end = int(lo * R), int(hi * R)
                while at < end:
                    whole = (end - at) // R if at % R == 0 else 0
                    if whole:
                        with t.Fori(0, whole) as i:
                            for r in range(R):
                                pick(b * PICKS + at + i * R + r, par, r)
                        at += whole * R
                    else:
                        pick(b * PICKS + at, par, at % R)
                        at += 1

            def tail(b, par):
                for r in TAIL:
                    pick(b * PICKS + GROUPS * R + r - TAIL[0], par, r, r == TAIL[-1])

            def transposes(dst, src):
                for k in range(KD):
                    ins = t.transpose(dst[:, k * P:(k + 1) * P], src[:, k * P:(k + 1) * P], ident[:, :])
                return ins

            def product(ends, dst, lhs, w, half):
                for k in range(KD):
                    ins = t.matmul(dst, lhs[:, k * P:(k + 1) * P], w[:, k, half * BANK:(half + 1) * BANK],
                                   start=k == 0, stop=k == KD - 1)
                if ends is not None:
                    ins.then_inc(ends, 1)

            def keep_x2(b, par):
                t.wait_ge(x2_ready, b + 1)
                if type(b) is not int:
                    t.wait_ge(y_norm, b - 1)
                for half in range(2):
                    ins = t.matmul(ACC[par][:, half * BANK:(half + 1) * BANK], ident[:, :],
                                   XC[:, half * BANK:(half + 1) * BANK], start=True, stop=False)
                ins.then_inc(x2_kept, 1)

            def final_rows(b):
                t.wait_ge(gf_diag, b + 1)
                for half in range(2):
                    ins = t.matmul(bank(4 + half), ones512[:, :], BC[:, half * BANK:(half + 1) * BANK],
                                   start=True, stop=True)
                ins.then_inc(gf_rows, 1)

            def attend(b, par, upto, at):
                upto(at["norm"])
                t.wait_ge(xa_norm, b + 1)
                transposes(PF[0], AC).then_inc(t1_done, 1)
                upto(at["sc"][0])
                t.wait_ge(h1_ready, b + 1)
                t.wait_ge(qk_load, 16 if type(b) is int else 32)
                product(None, bank(6), BC, qk, 0)
                upto(at["sc"][1])
                product(sc_done, bank(7), BC, qk, 1)
                upto(at["soft"])
                t.wait_ge(pn_ready, b + 1)
                transposes(PF[0], BC).then_inc(pt_done, 1)
                upto(at["xo"][0])
                t.wait_ge(pt_ready, b + 1)
                t.wait_ge(vo_load, 16 if type(b) is int else 32)
                product(None, bank(6), AC, vo, 0)
                upto(at["xo"][1])
                product(xo_done, bank(7), AC, vo, 1)
                upto(at["x2"])
                keep_x2(b, par)
                upto(at["tr"])
                t.wait_ge(xp_norm, b + 1)
                transposes(PF[0], AC).then_inc(t2_done, 1)
                t.wait_ge(h2_ready, b + 1)
                transposes(PF[1], BC).then_inc(t3_done, 1)

            def score(b, upto, at, lo, hi):
                for q in range(lo, hi):
                    upto(at["q"][q])
                    if type(b) is int and b == 0:
                        t.wait_ge(wpa_load if q < 2 else wpb_load, 16)
                    if q == 2:
                        t.wait_ge(h_ready, b + 1)
                    product(s_done, bank(4 + q), BC, wp[q // 2], q % 2)

            def mixer():
                left = sorted(MIX_TURN)

                def upto(turn):
                    while left and MIX_TURN[left[0]] < turn:
                        mix_out(left.pop(0))
                return upto

            def walker(b, par):
                pos = [0]

                def upto(turn):
                    if turn > pos[0]:
                        walk(b, par, pos[0], turn)
                        pos[0] = turn
                return upto

            upto = mixer()
            attend(0, 0, upto, FIRST)
            score(0, upto, FIRST, 0, 1)
            upto(GROUPS)
            t.sem_inc(row_used, R)
            upto = walker(0, 0)
            score(0, upto, FIRST, 1, Q)
            t.wait_ge(out_took, 4 * NB)
            attend(1, 1, upto, SECOND)
            score(1, upto, SECOND, 0, Q)
            upto(GROUPS)
            tail(0, 0)
            with t.Fori(0, (NB - 2) // 2) as pair:
                for par in (1, 0):
                    b = pair * 2 + (2 - par)
                    upto = walker(b, par)
                    upto(1)
                    final_rows(b - 1)
                    attend(b + 1, 1 - par, upto, STEADY)
                    score(b + 1, upto, STEADY, 0, Q)
                    upto(GROUPS)
                    tail(b, par)
            walk(NB - 1, 1, 0, 1)
            final_rows(NB - 2)
            walk(NB - 1, 1, 1, 3)
            final_rows(NB - 1)
            walk(NB - 1, 1, 3, GROUPS)
            tail(NB - 1, 1)


def kernel(**inputs):
    import numpy as np
    import concourse.bacc as bacc
    from concourse.bass_utils import run_bass_kernel_spmd as run

    x = {k: np.asarray(v) for k, v in inputs.items()}
    nc = bacc.Bacc("TRN2", target_bir_lowering=False, num_devices=1)

    def channels(w):
        return w.reshape(-1, P).T

    cols = np.concatenate([channels(x[k][0]) for k in (
        "g_mix", "g_mem", "g_xattn", "g_peer", "conv4_w", "conv4_b", "lru_ba", "lru_bx", "lru_lam",
        "conv31_w", "conv31_b", "conv_ln_g", "conv_ln_b", "g_out_rnn", "g_out_conv")]
        + [channels(x["g_final"])], axis=1)

    def stationary(w):
        return w.reshape(KD, P, -1, P).transpose(2, 1, 0, 3).reshape(-1, P, D)

    w_in = stationary(x["w_in"][0])[[BASE[k] + c for k, c in CHUNKS]]
    w_k = stationary(x["w_xkv"][0][:, :D])
    w_v = stationary(x["w_xkv"][0][:, D:])
    w_q = x["w_xq"][0].T.reshape(KD, P, D)
    w_o = x["w_xo"][0].reshape(KD, P, D)
    w_pq = x["w_pq"][0].T.reshape(2 * PH, P, D)

    def paired(w):
        return w.reshape(-1, 2, P, D).transpose(0, 2, 1, 3).reshape(-1, P, 2 * D)

    items = {kind: paired(w) for kind, w in (("z", w_in), ("k", w_k), ("qk", w_q), ("v", w_v), ("vo", w_o), ("w", w_pq))}
    items = np.stack(list(items["z"]) + [items[kind][i] for kind, i in B_ITEMS])
    gates = np.stack([x["lru_wa"][0], x["lru_wx"][0]]).reshape(2, 2, CH, 2, 64, 64)\
        .transpose(3, 4, 0, 1, 2, 5).reshape(2, 64, 16, 64)
    arrays = {
        "xm": np.concatenate([x["x_prompt"][0], x["x_sample"][0], x["mem_prompt"][0], x["mem_sample"][0]]),
        "cols": cols, "items": items, "gates": gates,
        "subk": x["peer_sub_keys"][0].reshape(2 * PH, NK, P).transpose(2, 0, 1),
        "w_out": x["w_out"][0],
        "uv": np.concatenate([x["peer_u"][0], x["peer_v"][0]], axis=1),
    }
    arrays = {f"in_{k}": np.ascontiguousarray(v) for k, v in arrays.items()}
    aps = {k[3:]: nc.dram_tensor(k, v.shape, mybir.dt.from_np(v.dtype), kind="ExternalInput").ap()
           for k, v in arrays.items()}
    aps["out"] = nc.dram_tensor("out_0", (T, D), mybir.dt.float32, kind="ExternalOutput").ap()
    build(nc, aps)
    y = run(nc, [arrays], core_ids=[0]).results[0]["out_0"]
    return y[None, :SEQ0], y[None, SEQ0:]
```
